# Optimizing a Trainium2 kernel written in Bass

```python
import jax
import jax.numpy as jnp
from jax import lax
import numpy as np
import jax, jax.numpy as jnp

D_MODEL = 1024
BATCH = 1
SEQ = 512
DEPTH = 1

D_RNN = D_MODEL
N_LRU_BLOCKS = 16
LRU_BLOCK = D_RNN // N_LRU_BLOCKS
CONV_WIDTH = 4
LRU_C = 8.0
N_HEADS = 16
HEAD_DIM = 64
N_KV_GROUPS = 4
HEADS_PER_GROUP = N_HEADS // N_KV_GROUPS
D_ATTN = N_HEADS * HEAD_DIM
D_KV = N_KV_GROUPS * HEAD_DIM
CMP_LEN = 32
CMP_STRIDE = 16
CMP_HIDDEN = 256
SEL_LEN = 64
SEL_TOPK = 16
WINDOW = 512
Q_BLOCK = 64
FORCE_SCORE = 1e4
R_SEL = SEL_LEN // CMP_STRIDE
R_CMP = CMP_LEN // CMP_STRIDE
ALIBI_MAX_BIAS = 8.0
D_FF = 2816
D_PLE = 256
NORM_EPS = 1e-6

_IN_SIZES = (D_RNN, D_RNN, D_ATTN, D_KV, D_KV, D_KV, D_KV, D_KV, D_KV, 3 * N_HEADS, D_MODEL, D_MODEL)
D_IN = sum(_IN_SIZES)
IN_SPLITS = tuple(int(c) for c in np.cumsum(_IN_SIZES)[:-1])


def rmsnorm(x, g):
    x32 = x.astype(jnp.float32)
    y = x32 * lax.rsqrt(jnp.mean(x32 * x32, axis=-1, keepdims=True) + NORM_EPS)
    return (y * g.astype(jnp.float32)).astype(x.dtype)

def alibi_slopes():
    h = jnp.arange(1, N_HEADS + 1, dtype=jnp.float32)
    return jnp.exp2(-ALIBI_MAX_BIAS * h / N_HEADS)

def masked_softmax(s, mask):
    s = jnp.where(mask, s.astype(jnp.float32), -jnp.inf)
    m = jnp.max(s, axis=-1, keepdims=True)
    m = jnp.where(jnp.isfinite(m), m, 0.0)
    e = jnp.where(mask, jnp.exp(s - m), 0.0)
    return e / jnp.maximum(jnp.sum(e, axis=-1, keepdims=True), 1e-30)

def causal_conv(x, w, b):
    S = x.shape[1]
    xp = jnp.pad(x, ((0, 0), (CONV_WIDTH - 1, 0), (0, 0)))
    y = b
    for k in range(CONV_WIDTH):
        y = y + xp[:, k:k + S] * w[k]
    return y

def _lru_combine(c1, c2):
    a1, b1 = c1
    a2, b2 = c2
    return a1 * a2, a2 * b1 + b2

def rg_lru(xc, wa, ba, wx, bx, lam):
    B, S, _ = xc.shape
    xb = xc.reshape(B, S, N_LRU_BLOCKS, LRU_BLOCK)
    r = jax.nn.sigmoid(jnp.einsum('bsnd,nde->bsne', xb, wa).reshape(B, S, D_RNN) + ba)
    i = jax.nn.sigmoid(jnp.einsum('bsnd,nde->bsne', xb, wx).reshape(B, S, D_RNN) + bx)
    log_a = (-LRU_C * r.astype(jnp.float32)) * jax.nn.softplus(-lam.astype(jnp.float32))
    a = jnp.exp(log_a)
    b = jnp.sqrt(-jnp.expm1(2.0 * log_a)) * (i * xc).astype(jnp.float32)
    _, h = lax.associative_scan(_lru_combine, (a, b), axis=1)
    return h.astype(xc.dtype)

def compress(kv, pos, w1, w2):
    B, S, G, dh = kv.shape
    c = kv.reshape(B, S // CMP_STRIDE, CMP_STRIDE, G, dh)
    blk = jnp.concatenate([c[:, :-1], c[:, 1:]], axis=2)
    blk = blk + pos[:, None, :]
    nc = blk.shape[1]
    blk = blk.transpose(0, 1, 3, 2, 4).reshape(B, nc, G, CMP_LEN * dh)
    return jax.nn.gelu(blk @ w1) @ w2

def nsa(q, kc, vc, ks, vs, kw, vw, gates, slopes):
    B, S = q.shape[0], q.shape[1]
    G, R, dh = N_KV_GROUPS, HEADS_PER_GROUP, HEAD_DIM
    NQ = S // Q_BLOCK
    NB = S // SEL_LEN
    NC = kc.shape[1]
    topk = min(SEL_TOPK, NB)
    scale = HEAD_DIM ** -0.5
    slopes_g = slopes.reshape(G, R)[None, :, :, None, None]
    cmp_end = jnp.arange(NC) * CMP_STRIDE + (CMP_LEN - 1)
    kc_t = kc.transpose(0, 2, 1, 3)
    vc_t = vc.transpose(0, 2, 1, 3)
    ks_blk = ks.reshape(B, NB, SEL_LEN, G, dh).transpose(0, 3, 1, 2, 4)
    vs_blk = vs.reshape(B, NB, SEL_LEN, G, dh).transpose(0, 3, 1, 2, 4)
    kw_pad = jnp.pad(kw, ((0, 0), (WINDOW, 0), (0, 0), (0, 0)))
    vw_pad = jnp.pad(vw, ((0, 0), (WINDOW, 0), (0, 0), (0, 0)))
    q_blocks = q.reshape(B, NQ, Q_BLOCK, G, R, dh).transpose(1, 0, 2, 3, 4, 5)
    g_blocks = gates.reshape(B, NQ, Q_BLOCK, G, R, 3).transpose(1, 0, 2, 3, 4, 5)
    gather = jax.vmap(jax.vmap(lambda kb, idx: kb[idx]))
    blk_ids = jnp.arange(NB)

    def one_block(args):
        qb, qi, gi = args
        q0 = qb * Q_BLOCK
        t = q0 + jnp.arange(Q_BLOCK)
        qf = qi * scale
        dist_c = t[:, None] - cmp_end[None, :]
        s = jnp.einsum('bqgrd,bgcd->bgrqc', qf, kc_t) - slopes_g * dist_c
        p_cmp = masked_softmax(s, dist_c >= 0)
        o_cmp = jnp.einsum('bgrqc,bgcd->bqgrd', p_cmp.astype(vc_t.dtype), vc_t)
        imp = jnp.sum(p_cmp, axis=2)
        left = R_CMP - 1
        imp = jnp.pad(imp, ((0, 0), (0, 0), (0, 0), (left, R_SEL * NB - NC)))
        imp_slc = jnp.zeros(imp.shape[:3] + (NB,), jnp.float32)
        for m in range(R_SEL):
            for n in range(R_CMP):
                st = m - n + left
                imp_slc = imp_slc + imp[..., st:st + R_SEL * NB:R_SEL]
        cur = t // SEL_LEN
        valid = blk_ids[None, :] * SEL_LEN <= t[:, None]
        forced = (blk_ids[None, :] == 0) | (blk_ids[None, :] == cur[:, None]) | (blk_ids[None, :] == cur[:, None] - 1)
        score = jnp.where(valid, imp_slc, -1.0)
        score = jnp.where(forced & valid, FORCE_SCORE, score)
        _, idx = lax.top_k(score, topk)
        k_sel = gather(ks_blk, idx).reshape(B, G, Q_BLOCK, topk * SEL_LEN, dh)
        v_sel = gather(vs_blk, idx).reshape(B, G, Q_BLOCK, topk * SEL_LEN, dh)
        pos = (idx[..., None] * SEL_LEN + jnp.arange(SEL_LEN)).reshape(B, G, Q_BLOCK, topk * SEL_LEN)
        dist_s = t[None, None, :, None] - pos
        s = jnp.einsum('bqgrd,bgqkd->bgrqk', qf, k_sel) - slopes_g * dist_s[:, :, None]
        p_sel = masked_softmax(s, (dist_s >= 0)[:, :, None])
        o_slc = jnp.einsum('bgrqk,bgqkd->bqgrd', p_sel.astype(v_sel.dtype), v_sel)
        kwin = lax.dynamic_slice_in_dim(kw_pad, q0, WINDOW + Q_BLOCK, axis=1)
        vwin = lax.dynamic_slice_in_dim(vw_pad, q0, WINDOW + Q_BLOCK, axis=1)
        pos_w = q0 - WINDOW + jnp.arange(WINDOW + Q_BLOCK)
        dist_w = t[:, None] - pos_w[None, :]
        mask_w = (dist_w >= 0) & (dist_w < WINDOW) & (pos_w[None, :] >= 0)
        s = jnp.einsum('bqgrd,bkgd->bgrqk', qf, kwin) - slopes_g * dist_w
        p_win = masked_softmax(s, mask_w)
        o_win = jnp.einsum('bgrqk,bkgd->bqgrd', p_win.astype(vwin.dtype), vwin)
        g = jax.nn.sigmoid(gi)
        return g[..., 0:1] * o_cmp + g[..., 1:2] * o_slc + g[..., 2:3] * o_win

    o = lax.map(one_block, (jnp.arange(NQ), q_blocks, g_blocks))
    return o.transpose(1, 0, 2, 3, 4, 5).reshape(B, S, D_ATTN)

def first_inputs(seed: int = 0) -> dict:
    key = jax.random.key(seed)
    ks = jax.random.split(key, 32)
    f32 = jnp.float32

    def nrm(k, shape, fan_in):
        return jax.random.normal(k, shape, f32) * (fan_in ** -0.5)

    def gain(k):
        return 1.0 + 0.05 * jax.random.normal(k, (DEPTH, D_MODEL), f32)

    u = jax.random.uniform(ks[10], (DEPTH, D_RNN), f32, minval=0.9, maxval=0.999)
    s = u ** (1.0 / LRU_C)
    lam = jnp.log(s) - jnp.log1p(-s)
    return {
        'x': jax.random.normal(ks[0], (BATCH, SEQ, D_MODEL), f32),
        'p': jax.random.normal(ks[1], (DEPTH, BATCH, SEQ, D_PLE), f32),
        'norm_mix_pre': gain(ks[2]),
        'norm_mix_post': gain(ks[3]),
        'w_in': nrm(ks[4], (DEPTH, D_MODEL, D_IN), D_MODEL),
        'conv_w': nrm(ks[5], (DEPTH, CONV_WIDTH, D_RNN), CONV_WIDTH),
        'conv_b': 0.02 * jax.random.normal(ks[6], (DEPTH, D_RNN), f32),
        'lru_wa': nrm(ks[7], (DEPTH, N_LRU_BLOCKS, LRU_BLOCK, LRU_BLOCK), LRU_BLOCK),
        'lru_ba': 0.02 * jax.random.normal(ks[8], (DEPTH, D_RNN), f32),
        'lru_wx': nrm(ks[9], (DEPTH, N_LRU_BLOCKS, LRU_BLOCK, LRU_BLOCK), LRU_BLOCK),
        'lru_bx': 0.02 * jax.random.normal(ks[11], (DEPTH, D_RNN), f32),
        'lru_lambda': lam,
        'cmp_pos_k': 0.02 * jax.random.normal(ks[12], (DEPTH, CMP_LEN, HEAD_DIM), f32),
        'cmp_pos_v': 0.02 * jax.random.normal(ks[13], (DEPTH, CMP_LEN, HEAD_DIM), f32),
        'cmp_k_w1': nrm(ks[14], (DEPTH, CMP_LEN * HEAD_DIM, CMP_HIDDEN), CMP_LEN * HEAD_DIM),
        'cmp_k_w2': nrm(ks[15], (DEPTH, CMP_HIDDEN, HEAD_DIM), CMP_HIDDEN),
        'cmp_v_w1': nrm(ks[16], (DEPTH, CMP_LEN * HEAD_DIM, CMP_HIDDEN), CMP_LEN * HEAD_DIM),
        'cmp_v_w2': nrm(ks[17], (DEPTH, CMP_HIDDEN, HEAD_DIM), CMP_HIDDEN),
        'w_out': nrm(ks[18], (DEPTH, D_MODEL, D_MODEL), D_MODEL),
        'norm_ffn_pre': gain(ks[19]),
        'norm_ffn_post': gain(ks[20]),
        'ffn_w_gate_up': nrm(ks[21], (DEPTH, D_MODEL, 2 * D_FF), D_MODEL),
        'ffn_w_down': nrm(ks[22], (DEPTH, D_FF, D_MODEL), D_FF),
        'ple_w_proj': nrm(ks[23], (DEPTH, D_PLE, D_MODEL), D_PLE),
        'ple_w_gate': nrm(ks[24], (DEPTH, D_MODEL, D_MODEL), D_MODEL),
        'ple_b_gate': 0.02 * jax.random.normal(ks[25], (DEPTH, D_MODEL), f32),
    }

def first_block(x, p, norm_mix_pre, norm_mix_post, w_in, conv_w, conv_b, lru_wa, lru_ba, lru_wx, lru_bx,
              lru_lambda, cmp_pos_k, cmp_pos_v, cmp_k_w1, cmp_k_w2, cmp_v_w1, cmp_v_w2, w_out,
              norm_ffn_pre, norm_ffn_post, ffn_w_gate_up, ffn_w_down, ple_w_proj, ple_w_gate, ple_b_gate):
    B, S, _ = x.shape
    slopes = alibi_slopes()
    for i in range(DEPTH):
        h = rmsnorm(x, norm_mix_pre[i])
        z = h @ w_in[i]
        xr, gr, q, kc, vc, ksl, vsl, kw, vw, g_nsa, gm_rnn, gm_attn = jnp.split(z, IN_SPLITS, axis=-1)
        xr = causal_conv(xr, conv_w[i], conv_b[i])
        y_rnn = rg_lru(xr, lru_wa[i], lru_ba[i], lru_wx[i], lru_bx[i], lru_lambda[i]) * jax.nn.gelu(gr)
        kv_shape = (B, S, N_KV_GROUPS, HEAD_DIM)
        kc_c = compress(kc.reshape(kv_shape), cmp_pos_k[i], cmp_k_w1[i], cmp_k_w2[i])
        vc_c = compress(vc.reshape(kv_shape), cmp_pos_v[i], cmp_v_w1[i], cmp_v_w2[i])
        y_attn = nsa(q, kc_c, vc_c, ksl.reshape(kv_shape), vsl.reshape(kv_shape),
                     kw.reshape(kv_shape), vw.reshape(kv_shape), g_nsa, slopes)
        y = jax.nn.sigmoid(gm_rnn) * y_rnn + jax.nn.sigmoid(gm_attn) * y_attn
        x = x + rmsnorm(y @ w_out[i], norm_mix_post[i])
        h = rmsnorm(x, norm_ffn_pre[i])
        gate, up = jnp.split(h @ ffn_w_gate_up[i], 2, axis=-1)
        x = x + rmsnorm((jax.nn.silu(gate) * up) @ ffn_w_down[i], norm_ffn_post[i])
        x = x + jax.nn.sigmoid(x @ ple_w_gate[i] + ple_b_gate[i]) * (p[i] @ ple_w_proj[i])
    return x


DEPTH_2 = 2

CTX_LEN = 256
GRID_W = 64
N_HEADS_2 = 8
N_KV_HEADS = 2
GQA = N_HEADS_2 // N_KV_HEADS
ATTN_WIDTH = N_HEADS_2 * HEAD_DIM
KV_WIDTH = N_KV_HEADS * HEAD_DIM
WINDOW_2 = 128
ATTN_BLOCK = 128
ATTN_SCALE = HEAD_DIM ** -0.5
ROPE_BASE = 10000.0
CONV_WIDTH_2 = D_MODEL // 4
GM_WIDTH = D_MODEL // 4
GM_GROUPS = 4
GM_HEAD = GM_WIDTH // GM_GROUPS
CHUNK = 128
MIX_WIDTH = ATTN_WIDTH + CONV_WIDTH_2 + GM_WIDTH
IN_WIDTH = ATTN_WIDTH + 2 * KV_WIDTH + 3 * CONV_WIDTH_2 + 2 * GM_WIDTH
SPLIT_POINTS = (ATTN_WIDTH,
                ATTN_WIDTH + KV_WIDTH,
                ATTN_WIDTH + 2 * KV_WIDTH,
                ATTN_WIDTH + 2 * KV_WIDTH + CONV_WIDTH_2,
                ATTN_WIDTH + 2 * KV_WIDTH + 2 * CONV_WIDTH_2,
                ATTN_WIDTH + 2 * KV_WIDTH + 3 * CONV_WIDTH_2,
                ATTN_WIDTH + 2 * KV_WIDTH + 3 * CONV_WIDTH_2 + GM_WIDTH)
N_GROUPS = 4
EXP_PER_GROUP = 8
N_EXPERTS = N_GROUPS * EXP_PER_GROUP
TOP_K = 2
D_EXPERT = D_MODEL // 2
MOE_BLOCK = 128
ALPHA = (2 * DEPTH_2) ** 0.25
BETA = (8 * DEPTH_2) ** -0.25
LN_EPS = 1e-6
NEG_INF = -1e30


def layer_norm(x, g=None, b=None):
    xf = x.astype(jnp.float32)
    mu = jnp.mean(xf, axis=-1, keepdims=True)
    var = jnp.mean(jnp.square(xf - mu), axis=-1, keepdims=True)
    y = (xf - mu) * lax.rsqrt(var + LN_EPS)
    if g is not None:
        y = y * g.astype(jnp.float32) + b.astype(jnp.float32)
    return y.astype(x.dtype)

def _rope(x, pos):
    m = x.shape[-1] // 2
    freqs = ROPE_BASE ** (-jnp.arange(m, dtype=jnp.float32) / m)
    ang = pos.astype(jnp.float32)[:, None] * freqs[None, :]
    cos = jnp.cos(ang)[None, :, None, :]
    sin = jnp.sin(ang)[None, :, None, :]
    xf = x.astype(jnp.float32)
    a, b = xf[..., :m], xf[..., m:]
    return jnp.concatenate([a * cos - b * sin, b * cos + a * sin], axis=-1).astype(x.dtype)

def axial_rope(x, row, col):
    half = x.shape[-1] // 2
    return jnp.concatenate([_rope(x[..., :half], row), _rope(x[..., half:], col)], axis=-1)

def short_conv(u, w):
    up = jnp.pad(u, ((0, 0), (1, 1), (0, 0)))
    return up[:, :-2] * w[0] + up[:, 1:-1] * w[1] + up[:, 2:] * w[2]

def local_mixers(cb, cc, cx, gu, gv, conv_w, gm_ws, gm_bs):
    y_conv = cb * short_conv(cc * cx, conv_w)
    b_, l_ = gu.shape[:2]
    u = jax.nn.gelu(gu)
    v = layer_norm(jax.nn.gelu(gv)).reshape(b_, l_ // CHUNK, CHUNK, GM_GROUPS, GM_HEAD)
    s = jnp.einsum('gpq,bnqgc->bnpgc', gm_ws, v) + gm_bs.T[None, None, :, :, None]
    y_gm = u * s.reshape(b_, l_, GM_WIDTH).astype(u.dtype)
    return jnp.concatenate([y_conv, y_gm], axis=-1)

def sink_softmax(s, sink):
    col = jnp.broadcast_to(sink.astype(jnp.float32).reshape(N_KV_HEADS, GQA)[None, :, :, None, None],
                           s.shape[:-1] + (1,))
    return jax.nn.softmax(jnp.concatenate([col, s], axis=-1), axis=-1)[..., 1:]

def window_attention(q, k, v, k_ctx, v_ctx, sink):
    b_, s_ = q.shape[:2]
    nb = s_ // ATTN_BLOCK
    pad = ((0, 0), (ATTN_BLOCK, ATTN_BLOCK), (0, 0), (0, 0))
    kp, vp = jnp.pad(k, pad), jnp.pad(v, pad)
    span = 3 * ATTN_BLOCK
    rel = (jnp.arange(span)[None, :] - ATTN_BLOCK) - jnp.arange(ATTN_BLOCK)[:, None]
    band = jnp.abs(rel) <= WINDOW_2

    def one_block(n):
        start = n * ATTN_BLOCK
        qn = lax.dynamic_slice_in_dim(q, start, ATTN_BLOCK, axis=1).reshape(
            b_, ATTN_BLOCK, N_KV_HEADS, GQA, HEAD_DIM)
        kn = lax.dynamic_slice_in_dim(kp, start, span, axis=1)
        vn = lax.dynamic_slice_in_dim(vp, start, span, axis=1)
        kpos = start - ATTN_BLOCK + jnp.arange(span)
        valid = band & ((kpos >= 0) & (kpos < s_))[None, :]
        s_loc = jnp.einsum('bqkgd,bskd->bkgqs', qn, kn, preferred_element_type=jnp.float32) * ATTN_SCALE
        s_loc = jnp.where(valid, s_loc, NEG_INF)
        s_ctx = jnp.einsum('bqkgd,bckd->bkgqc', qn, k_ctx, preferred_element_type=jnp.float32) * ATTN_SCALE
        p = sink_softmax(jnp.concatenate([s_loc, s_ctx], axis=-1), sink).astype(v.dtype)
        o = (jnp.einsum('bkgqs,bskd->bqkgd', p[..., :span], vn)
             + jnp.einsum('bkgqc,bckd->bqkgd', p[..., span:], v_ctx))
        return o.reshape(b_, ATTN_BLOCK, ATTN_WIDTH)

    out = lax.map(one_block, jnp.arange(nb))
    return out.transpose(1, 0, 2, 3).reshape(b_, s_, ATTN_WIDTH)

def context_attention(q, k, v, sink):
    b_, c_ = q.shape[:2]
    qg = q.reshape(b_, c_, N_KV_HEADS, GQA, HEAD_DIM)
    s = jnp.einsum('bqkgd,bckd->bkgqc', qg, k, preferred_element_type=jnp.float32) * ATTN_SCALE
    p = sink_softmax(s, sink).astype(v.dtype)
    o = jnp.einsum('bkgqc,bckd->bqkgd', p, v)
    return o.reshape(b_, c_, ATTN_WIDTH)

def hier_moe(h, w_rg, b_rg, w_re, b_re, w1, w3, w2):
    n, d_ = h.shape
    hf = h.astype(jnp.float32)
    g_logit = hf @ w_rg.astype(jnp.float32) + b_rg.astype(jnp.float32)
    g_val, g_idx = lax.top_k(g_logit, 1)
    p_group = jnp.exp(g_val[:, 0] - jax.nn.logsumexp(g_logit, axis=-1))
    e_logit = (hf @ w_re.astype(jnp.float32)).reshape(n, N_GROUPS, EXP_PER_GROUP) \
        + b_re.astype(jnp.float32).reshape(N_GROUPS, EXP_PER_GROUP)
    e_logit = jnp.take_along_axis(e_logit, g_idx[:, :, None], axis=1)[:, 0]
    e_val, e_idx = lax.top_k(e_logit, TOP_K)
    gates = p_group[:, None] * jax.nn.softmax(e_val, axis=-1)
    expert = g_idx * EXP_PER_GROUP + e_idx

    a = n * TOP_K
    flat_e = expert.reshape(-1)
    flat_g = gates.reshape(-1)
    order = jnp.argsort(flat_e)
    se = flat_e[order]
    counts = jnp.bincount(flat_e, length=N_EXPERTS)
    starts = jnp.cumsum(counts) - counts
    padded = (counts + MOE_BLOCK - 1) // MOE_BLOCK * MOE_BLOCK
    pends = jnp.cumsum(padded)
    pstarts = pends - padded
    dest = pstarts[se] + jnp.arange(a) - starts[se]
    n_blocks = -(-a // MOE_BLOCK) + N_EXPERTS
    slot_tok = jnp.zeros(n_blocks * MOE_BLOCK, jnp.int32).at[dest].set((order // TOP_K).astype(jnp.int32))
    slot_gate = jnp.zeros(n_blocks * MOE_BLOCK, h.dtype).at[dest].set(flat_g[order].astype(h.dtype))
    block_e = jnp.minimum(jnp.searchsorted(pends, jnp.arange(n_blocks) * MOE_BLOCK, side='right'),
                          N_EXPERTS - 1)
    xs = h[slot_tok].reshape(n_blocks, MOE_BLOCK, d_)

    def run(args):
        xb, e = args
        return (jax.nn.silu(xb @ w1[e]) * (xb @ w3[e])) @ w2[e]

    ys = lax.map(run, (xs, block_e)).reshape(-1, d_)
    return jnp.zeros_like(h).at[slot_tok].add(ys * slot_gate[:, None])

def second_inputs(seed: int = 0) -> dict:
    key = jax.random.key(seed)
    ks = jax.random.split(key, 23)

    def nrm(k, shape, s):
        return jax.random.normal(k, shape, jnp.float32) * s

    d = D_MODEL
    return {
        'x': nrm(ks[0], (BATCH, SEQ, d), 1.0),
        'c': nrm(ks[1], (BATCH, d), 1.0),
        'ctx': nrm(ks[2], (BATCH, CTX_LEN, d), 1.0),
        'c_ctx': nrm(ks[3], (d,), 1.0),
        'w_ada': nrm(ks[4], (DEPTH_2, d, 6 * d), d ** -0.5),
        'b_ada': nrm(ks[5], (DEPTH_2, 6 * d), 0.02),
        'w_in': nrm(ks[6], (DEPTH_2, d, IN_WIDTH), d ** -0.5),
        'conv_w': nrm(ks[7], (DEPTH_2, 3, CONV_WIDTH_2), 3 ** -0.5),
        'attn_sink': nrm(ks[8], (DEPTH_2, N_HEADS_2), 0.5),
        'gm_ws': nrm(ks[9], (DEPTH_2, GM_GROUPS, CHUNK, CHUNK), CHUNK ** -0.5),
        'gm_bs': 1.0 + nrm(ks[10], (DEPTH_2, GM_GROUPS, CHUNK), 0.02),
        'w_out': nrm(ks[11], (DEPTH_2, MIX_WIDTH, d), BETA * MIX_WIDTH ** -0.5),
        'ln1_g': 1.0 + nrm(ks[12], (DEPTH_2, d), 0.02),
        'ln1_b': nrm(ks[13], (DEPTH_2, d), 0.02),
        'w_rg': nrm(ks[14], (DEPTH_2, d, N_GROUPS), d ** -0.5),
        'b_rg': nrm(ks[15], (DEPTH_2, N_GROUPS), 0.01),
        'w_re': nrm(ks[16], (DEPTH_2, d, N_EXPERTS), d ** -0.5),
        'b_re': nrm(ks[17], (DEPTH_2, N_EXPERTS), 0.01),
        'w1': nrm(ks[18], (DEPTH_2, N_EXPERTS, d, D_EXPERT), d ** -0.5),
        'w3': nrm(ks[19], (DEPTH_2, N_EXPERTS, d, D_EXPERT), d ** -0.5),
        'w2': nrm(ks[20], (DEPTH_2, N_EXPERTS, D_EXPERT, d), BETA * D_EXPERT ** -0.5),
        'ln2_g': 1.0 + nrm(ks[21], (DEPTH_2, d), 0.02),
        'ln2_b': nrm(ks[22], (DEPTH_2, d), 0.02),
    }

def second_block(x, c, ctx, c_ctx, w_ada, b_ada, w_in, conv_w, attn_sink, gm_ws, gm_bs, w_out,
              ln1_g, ln1_b, w_rg, b_rg, w_re, b_re, w1, w3, w2, ln2_g, ln2_b):
    b_, s_, d_ = x.shape
    c_len = ctx.shape[1]
    rows = s_ // GRID_W
    row = jnp.repeat(jnp.arange(rows), GRID_W)
    col = jnp.tile(jnp.arange(GRID_W), rows)
    c_act = jax.nn.silu(c)
    cc_act = jax.nn.silu(c_ctx)

    for l in range(DEPTH_2):
        last = l == DEPTH_2 - 1
        mod_x = c_act @ w_ada[l] + b_ada[l]
        sh1, sc1, g1, sh2, sc2, g2 = jnp.split(mod_x[:, None, :], 6, axis=-1)
        n_mod = 2 if last else 6
        mod_c = (cc_act @ w_ada[l][:, :n_mod * d_] + b_ada[l][:n_mod * d_]).reshape(n_mod, d_)

        hx = x * (1 + sc1) + sh1
        hc = ctx * (1 + mod_c[1]) + mod_c[0]
        qx, kx, vx, cbx, ccx, cvx, gux, gvx = jnp.split(hx @ w_in[l], SPLIT_POINTS, axis=-1)
        qx = axial_rope(qx.reshape(b_, s_, N_HEADS_2, HEAD_DIM), row, col)
        kx = axial_rope(kx.reshape(b_, s_, N_KV_HEADS, HEAD_DIM), row, col)
        vx = vx.reshape(b_, s_, N_KV_HEADS, HEAD_DIM)
        if last:
            kc, vc = jnp.split(hc @ w_in[l][:, ATTN_WIDTH:ATTN_WIDTH + 2 * KV_WIDTH], 2, axis=-1)
        else:
            qc, kc, vc, cbc, ccc, cvc, guc, gvc = jnp.split(hc @ w_in[l], SPLIT_POINTS, axis=-1)
        kc = kc.reshape(b_, c_len, N_KV_HEADS, HEAD_DIM)
        vc = vc.reshape(b_, c_len, N_KV_HEADS, HEAD_DIM)

        att_x = window_attention(qx, kx, vx, kc, vc, attn_sink[l])
        o_x = jnp.concatenate(
            [att_x, local_mixers(cbx, ccx, cvx, gux, gvx, conv_w[l], gm_ws[l], gm_bs[l])], axis=-1) @ w_out[l]
        if not last:
            att_c = context_attention(qc, kc, vc, attn_sink[l])
            o_c = jnp.concatenate(
                [att_c, local_mixers(cbc, ccc, cvc, guc, gvc, conv_w[l], gm_ws[l], gm_bs[l])], axis=-1) @ w_out[l]
            ctx = layer_norm(ALPHA * ctx + mod_c[2] * o_c, ln1_g[l], ln1_b[l])
        x = layer_norm(ALPHA * x + g1 * o_x, ln1_g[l], ln1_b[l])

        hx = (x * (1 + sc2) + sh2).reshape(b_ * s_, d_)
        if last:
            tokens = hx
        else:
            hc = (ctx * (1 + mod_c[4]) + mod_c[3]).reshape(b_ * c_len, d_)
            tokens = jnp.concatenate([hx, hc], axis=0)
        y = hier_moe(tokens, w_rg[l], b_rg[l], w_re[l], b_re[l], w1[l], w3[l], w2[l])
        if not last:
            ctx = layer_norm(ALPHA * ctx + mod_c[5] * y[b_ * s_:].reshape(b_, c_len, d_), ln2_g[l], ln2_b[l])
        x = layer_norm(ALPHA * x + g2 * y[:b_ * s_].reshape(b_, s_, d_), ln2_g[l], ln2_b[l])

    return x


def setup_inputs(seed=0):
    out = dict(first_inputs(seed))
    for name, value in second_inputs(seed + 1).items():
        if name != "x":
            out[name + "_2"] = value
    return out


def reference(
    x, p, norm_mix_pre, norm_mix_post, w_in, conv_w, conv_b, lru_wa, lru_ba, lru_wx, lru_bx,
    lru_lambda, cmp_pos_k, cmp_pos_v, cmp_k_w1, cmp_k_w2, cmp_v_w1, cmp_v_w2, w_out,
    norm_ffn_pre, norm_ffn_post, ffn_w_gate_up, ffn_w_down, ple_w_proj, ple_w_gate, ple_b_gate,
    c_2, ctx_2, c_ctx_2, w_ada_2, b_ada_2, w_in_2, conv_w_2, attn_sink_2, gm_ws_2, gm_bs_2,
    w_out_2, ln1_g_2, ln1_b_2, w_rg_2, b_rg_2, w_re_2, b_re_2, w1_2, w3_2, w2_2, ln2_g_2,
    ln2_b_2,
):
    x = first_block(
        x, p, norm_mix_pre, norm_mix_post, w_in, conv_w, conv_b, lru_wa, lru_ba, lru_wx, lru_bx,
        lru_lambda, cmp_pos_k, cmp_pos_v, cmp_k_w1, cmp_k_w2, cmp_v_w1, cmp_v_w2, w_out,
        norm_ffn_pre, norm_ffn_post, ffn_w_gate_up, ffn_w_down, ple_w_proj, ple_w_gate,
        ple_b_gate,
    )
    return second_block(
        x, c_2, ctx_2, c_ctx_2, w_ada_2, b_ada_2, w_in_2, conv_w_2, attn_sink_2, gm_ws_2,
        gm_bs_2, w_out_2, ln1_g_2, ln1_b_2, w_rg_2, b_rg_2, w_re_2, b_re_2, w1_2, w3_2, w2_2,
        ln2_g_2, ln2_b_2,
    )


_drawn_inputs = setup_inputs


def setup_inputs(seed=0):
    import zlib

    import numpy as np

    out = dict(_drawn_inputs(seed))
    spreads = {}
    factors = {'lru_ba': 7.438,
     'lru_bx': 5.674,
     'cmp_pos_k': 26.358,
     'cmp_pos_v': 3.229,
     'ple_b_gate': 23.205,
     'attn_sink_2': 46.497,
     'gm_bs_2': 23.555,
     'b_rg_2': 5.25,
     'b_re_2': 15.719,
     'ctx_2': 3.009}
    for name, (base, spread) in spreads.items():
        noise = np.random.default_rng([zlib.crc32(name.encode()), seed]).standard_normal(out[name].shape)
        drawn = base * np.exp(spread * noise) if base else spread * noise
        out[name] = jnp.asarray(drawn.astype(out[name].dtype))
    for name, factor in factors.items():
        out[name] = (out[name] * factor).astype(out[name].dtype)
    return out
```

```python
from contextlib import ExitStack, contextmanager

import numpy as np

import concourse.bass as bass
from concourse import mybir

P = 128
F32 = mybir.dt.float32
U32 = mybir.dt.uint32
ALU = mybir.AluOpType
ACT = mybir.ActivationFunctionType
AX = mybir.AxisListType.X

D = 1024
KT = D // P
S = 512
ST = S // P
NHEAD, HD, NGRP = 16, 64, 4
NCMP = S // 16 - 1
CPAD = 32
FF = 2816
FT = FF // P
CONV = 4
LRU_C = 8.0
EPS = 1e-6
MIX_ORDER = [h for t in range(KT) for h in (8 * (t // 4) + t % 4, 8 * (t // 4) + 4 + t % 4)]
CAUSAL = ((3, 0, 512), (2, 512, 384), (0, 896, 128), (1, 1024, 256))
NCAUSAL = 1280
PT_AT = {0: 0, 1: 512, 3: 896, 2: 1024}

C = 256
T = S + C
TT = T // P
NL = 2
H2, KV2 = 8, 2
NEXP, NEG, EPG = 32, 4, 8
DE = 512
CAP = 96
ALPHA = (2 * NL) ** 0.25
NEGV = -1e30

VECS = ["g_mix_pre", "g_mix_post", "g_ffn_pre", "g_ffn_post", "ple_b", "conv0", "conv1", "conv2",
        "conv3", "conv_b", "lru_ba", "lru_bx", "lru_lam", "ln1_g0", "ln1_b0", "ln2_g0", "ln2_b0",
        "ln1_g1", "ln1_b1", "ln2_g1", "ln2_b1"]


class Signal:

    def __init__(self, sem):
        self.sem, self.base = sem, 0

    def wait(self, eng, n):
        eng.wait_ge(self.sem, n + self.base)

    def passed(self, n):
        self.base += n


class Ring:

    SLOTS = 6
    WORDS = 4096

    def __init__(self, nc, ctx, chunks):
        self.buf = ctx.enter_context(nc.sbuf_tensor("weight_ring", [P, self.SLOTS, self.WORDS], F32))
        self.landed = [ctx.enter_context(nc.semaphore(f"weights_landed{s}")) for s in range(self.SLOTS)]
        self.chunks, self.loads, self.uses = chunks, 0, 0
        self.last_use = {}

    def view(self, n, words=None):
        return self.buf[:, n % self.SLOTS, 0:words or self.WORDS]

    def feed(self, sp, upto):
        while self.loads < min(upto, len(self.chunks)):
            n, src = self.loads, self.chunks[self.loads]
            words = int(np.prod(src.shape[1:]))
            dst = self.view(n, words)
            if len(src.shape) == 3:
                dst = dst.rearrange("p (a b) -> p a b", a=src.shape[1])
            if n >= self.SLOTS:
                sp.wait_ge(*self.last_use[n - self.SLOTS])
            sp.dma_start(dst, src).then_inc(self.landed[n % self.SLOTS], 16)
            self.loads += 1

    def take(self, pe, words=None):
        n = self.uses
        pe.wait_ge(self.landed[n % self.SLOTS], 16 * (n // self.SLOTS + 1))
        self.uses += 1
        return self.view(n, words)

    def used(self, sem, value):
        self.last_use[self.uses - 1] = (sem, value)


class Core:

    stat_count = 0


def prime(c, signals):
    with c.nc.Block(no_gpsimd_drain=True) as block:

        @block.sync
        def _(sp):
            for s in signals:
                sp.sem_inc(s.sem, 1)
    for s in signals:
        s.passed(1)


@contextmanager
def stat_buffers(c):
    with ExitStack() as ctx:
        c.stat_count = c.stat_count + 1
        c.rstd, c.rstd_sq, c.stat = (ctx.enter_context(c.nc.sbuf_tensor(f"{n}{c.stat_count}", [P, T], F32))
                                     for n in ("rstd", "rstd_squared", "stat"))
        c.mean_w = ctx.enter_context(c.nc.sbuf_tensor(f"mean_weights{c.stat_count}", [P, P], F32))
        with c.nc.Block(no_gpsimd_drain=True) as block:

            @block.vector
            def _(dve):
                c.nc.vector.memset(c.mean_w[:, :], 1.0 / D)
                if c.stat_count == 1:
                    c.nc.vector.memset(c.ones[:, :], 1.0)
        yield


def project(nc, out, weights, rhs, tiles=KT):
    for k in range(tiles):
        last = nc.tensor.matmul(out, weights[:, k * P:(k + 1) * P], rhs(k), start=(k == 0), stop=(k == tiles - 1))
    return last


def norm_and_start(c, ios):
    nc, X, H = c.nc, c.X, c.H
    with ExitStack() as ctx:
        sq = ctx.enter_context(nc.sbuf_tensor("x_squared", [P, KT, S], F32))
        with nc.Block(no_gpsimd_drain=True) as block:

            @block.sync
            def _(sp):
                sp.dma_start(X[:, :, 0:S], ios["xT"].rearrange("(k p) t -> p k t", p=P)).then_inc(c.x_landed, 16)
                for dst, src in c.const_loads:
                    sp.dma_start(dst, src).then_inc(c.consts_landed, 16)
                c.ring.feed(sp, Ring.SLOTS)
        rms_scale(c, X[:, :, 0:S], sq, S, first=True)
        scale_by(c, H, X[:, :, 0:S], "g_mix_pre")


def rms_scale(c, src, sq, n, first=False):
    nc, ph = c.nc, c.ph
    banks = [(b, at, min(512, n - at)) for b, at in enumerate(range(0, n, 512))]
    with nc.Block(no_gpsimd_drain=True) as block:

        @block.scalar
        def _(act):
            if first:
                act.wait_ge(c.x_landed, 16)
            nc.scalar.activation(sq[:, :, 0:n], src, ACT.Square).then_inc(ph[0].sem, 1)
            ph[3].wait(act, 1)
            nc.scalar.activation(c.rstd[:, 0:n], c.rstd_sq[:, 0:n], ACT.Sqrt)

        @block.vector
        def _(dve):
            ph[0].wait(dve, 1)
            nc.vector.tensor_reduce(c.stat[:, 0:n], sq[:, :, 0:n].rearrange("p k t -> p t k"), AX, ALU.add)\
                .then_inc(ph[1].sem, 1)
            ph[2].wait(dve, 1)
            for b, at, w in banks:
                nc.vector.tensor_scalar(c.stat[:, at:at + w], c.ps[:, b, 0:w], EPS, None, ALU.add)
            dve.drain()
            nc.vector.reciprocal(c.rstd_sq[:, 0:n], c.stat[:, 0:n]).then_inc(ph[3].sem, 1)

        @block.tensor
        def _(pe):
            ph[1].wait(pe, 1)
            for b, at, w in banks:
                last = nc.tensor.matmul(c.ps[:, b, 0:w], c.mean_w[:, :], c.stat[:, at:at + w], start=True, stop=True)
            last.then_inc(ph[2].sem, 1)
    for s in ph[0:4]:
        s.passed(1)


def scale_by(c, out, src, gain, add_to=None):
    nc, ph = c.nc, c.ph
    with nc.Block(no_gpsimd_drain=True) as block:

        @block.vector
        def _(dve):
            if gain == "g_mix_pre":
                dve.wait_ge(c.consts_landed, 16 * len(c.const_loads))
            for k in range(KT):
                nc.vector.scalar_tensor_tensor(out=out[:, k, :], in0=src[:, k, :], scalar=c.vec(gain, k),
                                               in1=c.rstd[:, 0:S], op0=ALU.mult, op1=ALU.mult)\
                    .then_inc(ph[0].sem, 1)

        @block.gpsimd
        def _(pool):
            if add_to is None:
                return
            for k in range(KT):
                ph[0].wait(pool, k + 1)
                nc.gpsimd.tensor_tensor(add_to[:, k, :], add_to[:, k, :], out[:, k, :], ALU.add)
            pool.drain()
    ph[0].passed(KT)


def recurrent_mixer(c):
    nc, H, Y, ps, ring = c.nc, c.H, c.Y, c.ps, c.ring
    with ExitStack() as ctx:
        def sb(name, shape):
            return ctx.enter_context(nc.sbuf_tensor(name, shape, F32))

        sem = c.sem
        XR = sb("xr_padded", [P, 2, CONV - 1 + S])
        XC = sb("xr_conv", [P, 2, S])
        GR = sb("gelu_gr", [P, 2, S])
        GM = sb("sigmoid_gm_rnn", [P, 2, S])
        R = sb("lru_r", [P, S])
        I = sb("lru_i", [P, S])
        A = sb("lru_a", [P, S])
        TH = sb("lru_tanh", [P, S])
        M = sb("lru_m", [P, S])
        B = sb("lru_b", [P, S])
        HS = sb("lru_h", [P, S])
        WG = sb("lru_gates_w", [P, 2, KT, P])
        lam = sb("lru_lam_tmp", [P, 6, KT])
        zeroed = sem("lru_w_zeroed")
        gates_w = sem("lru_gates_w_landed")
        lam_v = sem("lru_lam_dve")
        lam_a = sem("lru_lam_act")
        z_ready = sem("rnn_z_ready")
        z_read = sem("rnn_z_read")
        xc_ready = sem("rnn_xc_ready")
        gates_ready = sem("rnn_gates_ready")
        gates_read = sem("rnn_gates_read")
        a_ready = sem("rnn_a_ready")
        m_ready = sem("rnn_m_ready")
        s_ready = sem("rnn_sqrt_ready")
        tile_done = sem("rnn_tile_done")
        with nc.Block(no_gpsimd_drain=True) as block:

            @block.gpsimd
            def _(pool):
                nc.gpsimd.memset(WG[:], 0.0).then_inc(zeroed, 1)

            @block.tensor
            def _(pe):
                for j in range(KT + 1):
                    if j < KT:
                        w = ring.take(pe, 3 * KT * P).rearrange("p (s w) -> p s w", s=3)
                        for s in range(3):
                            if 3 * j + s >= 6:
                                pe.wait_ge(z_read, 3 * j + s - 5)
                            last = project(nc, ps[:, (3 * j + s) % 6, :], w[:, s], lambda k: H[:, k, :])
                            last.then_inc(z_ready, 1)
                        ring.used(z_ready, 3 * j + 3)
                    if j >= 1:
                        if j == 1:
                            pe.wait_ge(gates_w, 64)
                        pe.wait_ge(xc_ready, j)
                        if j >= 2:
                            pe.wait_ge(gates_read, j - 1)
                        nc.tensor.matmul(ps[:, 6, :], WG[:, 0, j - 1, :], XC[:, (j - 1) % 2, :], start=True, stop=True)
                        nc.tensor.matmul(ps[:, 7, :], WG[:, 1, j - 1, :], XC[:, (j - 1) % 2, :], start=True, stop=True)\
                            .then_inc(gates_ready, 1)

            @block.scalar
            def _(act):
                act.wait_ge(lam_v, 1)
                nc.scalar.activation(lam[:, 1, :], lam[:, 0, :], ACT.Exp)
                act.drain()
                nc.scalar.activation(lam[:, 2, :], lam[:, 1, :], ACT.Ln, bias=c.ones[:, 0:1]).then_inc(lam_a, 1)
                for j in range(KT + 1):
                    if j < KT:
                        act.wait_ge(z_ready, 3 * j + 1)
                        if j >= 2:
                            act.wait_ge(xc_ready, j - 1)
                        nc.scalar.copy(XR[:, j % 2, CONV - 1:], ps[:, 3 * j % 6, :]).then_inc(z_read, 1)
                        act.wait_ge(z_ready, 3 * j + 2)
                        if j >= 2:
                            act.wait_ge(tile_done, j - 1)
                        nc.scalar.activation(GR[:, j % 2, :], ps[:, (3 * j + 1) % 6, :], ACT.Gelu_apprx_tanh)\
                            .then_inc(z_read, 1)
                        act.wait_ge(z_ready, 3 * j + 3)
                        nc.scalar.activation(GM[:, j % 2, :], ps[:, (3 * j + 2) % 6, :], ACT.Sigmoid)\
                            .then_inc(z_read, 1)
                    if j >= 1:
                        i = j - 1
                        act.wait_ge(gates_ready, j)
                        if i >= 1:
                            act.wait_ge(tile_done, i)
                        nc.scalar.activation(R[:, :], ps[:, 6, :], ACT.Sigmoid, bias=c.vec("lru_ba", i))
                        nc.scalar.activation(I[:, :], ps[:, 7, :], ACT.Sigmoid, bias=c.vec("lru_bx", i))\
                            .then_inc(gates_read, 1)
                        act.drain()
                        if i == 0:
                            act.wait_ge(lam_v, 2)
                        nc.scalar.activation(A[:, :], R[:, :], ACT.Exp, scale=lam[:, 4, i:i + 1])
                        nc.scalar.activation(TH[:, :], R[:, :], ACT.Tanh, scale=lam[:, 5, i:i + 1])\
                            .then_inc(a_ready, 1)
                        act.wait_ge(m_ready, j)
                        nc.scalar.activation(B[:, :], M[:, :], ACT.Sqrt).then_inc(s_ready, 1)

            @block.vector
            def _(dve):
                v = nc.vector
                v.tensor_scalar(lam[:, 3, :], c.vecs[:, VECS.index("lru_lam"), :], -1.0, None, ALU.mult)
                dve.drain()
                v.tensor_tensor(lam[:, 0, :], lam[:, 3, :], c.vecs[:, VECS.index("lru_lam"), :], ALU.min)\
                    .then_inc(lam_v, 1)
                v.memset(XR[:, :, 0:CONV - 1], 0.0)
                dve.wait_ge(lam_a, 1)
                v.scalar_tensor_tensor(out=lam[:, 1, :], in0=lam[:, 3, :], scalar=0.0, in1=lam[:, 2, :],
                                       op0=ALU.max, op1=ALU.add)
                dve.drain()
                v.tensor_scalar(lam[:, 4, :], lam[:, 1, :], -LRU_C, None, ALU.mult)
                v.tensor_scalar(lam[:, 5, :], lam[:, 1, :], LRU_C, None, ALU.mult).then_inc(lam_v, 1)
                for j in range(KT + 1):
                    if j < KT:
                        dve.wait_ge(z_read, 3 * j + 1)
                        if j >= 2:
                            dve.wait_ge(gates_ready, j - 1)
                        xr, xc = XR[:, j % 2, :], XC[:, j % 2, :]
                        v.tensor_scalar(xc, xr[:, 0:S], c.vec("conv0", j), c.vec("conv_b", j), ALU.mult, ALU.add)
                        for t in range(1, CONV):
                            dve.drain()
                            last = v.scalar_tensor_tensor(out=xc, in0=xr[:, t:t + S], scalar=c.vec(f"conv{t}", j),
                                                          in1=xc, op0=ALU.mult, op1=ALU.add)
                        last.then_inc(xc_ready, 1)
                    if j >= 1:
                        i = j - 1
                        dve.wait_ge(a_ready, j)
                        v.tensor_tensor(HS[:, :], A[:, :], A[:, :], ALU.mult)
                        dve.drain()
                        v.scalar_tensor_tensor(out=M[:, :], in0=HS[:, :], scalar=1.0, in1=TH[:, :],
                                               op0=ALU.add, op1=ALU.mult).then_inc(m_ready, 1)
                        v.tensor_tensor(I[:, :], I[:, :], XC[:, i % 2, :], ALU.mult)
                        dve.wait_ge(s_ready, j)
                        dve.drain()
                        v.tensor_tensor(B[:, :], B[:, :], I[:, :], ALU.mult)
                        dve.drain()
                        v.tensor_tensor_scan(HS[:, :], A[:, :], B[:, :], 0.0, ALU.mult, ALU.add)
                        v.tensor_tensor(GR[:, i % 2, :], GR[:, i % 2, :], GM[:, i % 2, :], ALU.mult)
                        dve.drain()
                        v.tensor_tensor(Y[:, i, :], HS[:, :], GR[:, i % 2, :], ALU.mult).then_inc(tile_done, 1)

            @block.sync
            def _(sp):
                sp.wait_ge(zeroed, 1)
                for g, w in enumerate((c.ios["lru_wa"], c.ios["lru_wx"])):
                    for h in range(2):
                        sp.dma_start(WG[64 * h:64 * h + 64, g, :, 64 * h:64 * h + 64],
                                     w.rearrange("(t h) d e -> h d t e", h=2)[h]).then_inc(gates_w, 16)
                ring.feed(sp, ring.uses + Ring.SLOTS)



def attention_inputs(c):
    nc, H, ps, ring, Q, KK = c.nc, c.H, c.ps, c.ring, c.Q, c.KK
    with ExitStack() as ctx:
        def sb(name, shape):
            return ctx.enter_context(nc.sbuf_tensor(name, shape, F32))

        KCV = sb("cmp_kv_in", [P, 4, S])
        KCS = sb("cmp_kv_swapped", [P, 4, S])
        XB = sb("cmp_blocks", [P, 16, P])
        POS = sb("cmp_pos", [P, 2, 16])
        W2 = sb("cmp_w2", [P, 2, 2, HD])
        HID = sb("cmp_hidden", [P, 2, 2, P])
        WGT = sb("gate_columns", [P, KT, 3 * NHEAD])
        small = c.sem("cmp_small_landed")
        z_ready, z_read = c.sem("att_z_ready"), c.sem("att_z_read")
        swapped = c.sem("cmp_swapped")
        xb_ready, hid_ready = c.sem("cmp_blocks_ready"), c.sem("cmp_hidden_ready")
        hid_act, cc_ready = c.sem("cmp_hidden_gelu"), c.sem("cmp_ready")
        xb_zero = c.sem("cmp_blocks_zeroed")
        gates_ready = c.sem("att_gates_ready")
        with nc.Block(no_gpsimd_drain=True) as block:

            @block.gpsimd
            def _(pool):
                nc.gpsimd.memset(XB[:], 0.0).then_inc(xb_zero, 1)

            @block.tensor
            def _(pe):
                u = 0
                for chunk in range(2):
                    w = ring.take(pe).rearrange("p (s w) -> p s w", s=4)
                    for s in range(4):
                        if u >= 6:
                            pe.wait_ge(z_read, u - 5)
                        project(nc, ps[:, u % 6, :], w[:, s], lambda k: H[:, k, :]).then_inc(z_ready, 1)
                        u += 1
                    ring.used(z_ready, u)
                w = ring.take(pe).rearrange("p (k n) -> p k n", k=KT)
                for i in range(ST):
                    pe.wait_ge(z_read, u - 5)
                    for k in range(KT):
                        last = nc.tensor.matmul(ps[:, u % 6, :], H[:, k, i * P:(i + 1) * P], w[:, k, :],
                                                start=(k == 0), stop=(k == KT - 1))
                    last.then_inc(z_ready, 1)
                    u += 1
                ring.used(z_ready, u)
                pe.wait_ge(small, 32)
                for i in range(ST):
                    for k in range(KT):
                        last = nc.tensor.matmul(ps[:, 6, i * 48:i * 48 + 48], H[:, k, i * P:(i + 1) * P],
                                                WGT[:, k, :], start=(k == 0), stop=(k == KT - 1))
                last.then_inc(gates_ready, 1)
                for chunk in range(2):
                    w = ring.take(pe).rearrange("p (s w) -> p s w", s=4)
                    for s in range(4):
                        pe.wait_ge(z_read, u - 5)
                        project(nc, ps[:, u % 6, :], w[:, s], lambda k: H[:, k, :]).then_inc(z_ready, 1)
                        u += 1
                    ring.used(z_ready, u)
                for b in range(2):
                    w = ring.take(pe).rearrange("p (l n) -> p l n", l=16)
                    pe.wait_ge(xb_ready, b + 1)
                    for m in range(2):
                        for l in range(16):
                            last = nc.tensor.matmul(ps[:, 7 - b, m * P:(m + 1) * P],
                                                    w[:, l, m * P:(m + 1) * P], XB[:, l, :],
                                                    start=(l == 0), stop=(l == 15))
                    last.then_inc(hid_ready, 1)
                    ring.used(hid_ready, b + 1)
                pe.wait_ge(hid_act, 2)
                pe.wait_ge(z_read, 20)
                for par in range(2):
                    for k in range(2):
                        nc.tensor.matmul(ps[64 * par:64 * par + 64, 0, 0:64].rearrange("p (a n) -> p a n", a=2),
                                         W2[:, 0, k, :],
                                         HID[:, 0, k, :].rearrange("p (a b n) -> p b a n", a=2, b=2)[:, par],
                                         start=(k == 0), stop=(k == 1))
                for k in range(2):
                    last = nc.tensor.matmul(ps[:, 1, 0:HD], HID[:, 1, k, :], W2[:, 1, k, :],
                                            start=(k == 0), stop=(k == 1))
                last.then_inc(cc_ready, 1)

            @block.sync
            def _(sp):
                sp.dma_start(POS[:, :, :], c.ios["cmp_pos"]).then_inc(small, 16)
                sp.dma_start(WGT[:, :, :], c.ios["w_gates"].rearrange("(k p) n -> p k n", p=P)).then_inc(small, 16)
                for b, name in enumerate(("k", "v")):
                    sp.dma_start(W2[:, b, :, :], c.ios[f"cmp_{name}_w2"].rearrange("(k p) n -> p k n", p=P))\
                        .then_inc(c.w2_landed, 16)
                ring.feed(sp, 8 + 6)
                sp.wait_ge(z_read, 4)
                for h in range(2):
                    sp.dma_start(KCS[64 * h:64 * h + 64, :, :], KCV[64 - 64 * h:128 - 64 * h, :, :])\
                        .then_inc(swapped, 16)
                ring.feed(sp, ring.uses + Ring.SLOTS)

            @block.scalar
            def _(act):
                for u in range(20):
                    act.wait_ge(z_ready, u + 1)
                    src = ps[:, u % 6, :]
                    if u < 4:
                        ins = nc.scalar.copy(KCV[:, u, :], src)
                    elif u < 8:
                        ins = nc.scalar.copy(KK[:, u - 4, :], src)
                    elif u < 12:
                        ins = nc.scalar.copy(c.V(u - 8), src.rearrange("p (b n) -> p b n", b=2))
                    else:
                        ins = nc.scalar.mul(Q[:, u - 12, :], src, HD ** -0.5)
                    ins.then_inc(z_read, 1)
                    if u == 12:
                        act.wait_ge(gates_ready, 1)
                        nc.scalar.activation(c.G[:, :, :], ps[:, 6, 0:4 * 48].rearrange("p (i n) -> p i n", i=4),
                                             ACT.Sigmoid)
                for b in range(2):
                    act.wait_ge(hid_ready, b + 1)
                    nc.scalar.activation(HID[:, b, :, :],
                                         ps[:, 7 - b, 0:2 * P].rearrange("p (m n) -> p m n", m=2),
                                         ACT.Gelu_apprx_tanh).then_inc(hid_act, 1)
                act.wait_ge(cc_ready, 1)
                nc.scalar.copy(c.KCC[:, :], ps[:, 0, 0:64])
                nc.scalar.copy(c.VCC[:, :], ps[:, 1, 0:HD])

            @block.vector
            def _(dve):
                dve.wait_ge(xb_zero, 1)
                dve.wait_ge(small, 32)
                dve.wait_ge(z_read, 4)
                dve.wait_ge(swapped, 32)
                for b in range(2):
                    if b:
                        dve.wait_ge(hid_ready, 1)
                    for h in range(2):
                        rows = slice(64 * h, 64 * h + 64)
                        for par in range(2):
                            src = (KCV if par == h else KCS)[rows, 2 * b:2 * b + 2, :]\
                                .rearrange("p a (n l e) -> p a n l e", l=8, e=2)[:, :, :, :, h]
                            dst = XB[rows, :, :].rearrange("p l (a b n) -> p b a n l", a=2, b=2)[:, par]
                            for q in range(2):
                                pos = POS[rows, b, 8 * q:8 * q + 8].unsqueeze(1).broadcast_to([64, NCMP, 8])
                                for a in range(2):
                                    last = nc.vector.tensor_tensor(dst[:, a, 0:NCMP, 8 * q:8 * q + 8],
                                                                   src[:, a, q:q + NCMP, :], pos, ALU.add)
                    last.then_inc(xb_ready, 1)


def compressed_probs(c):
    nc, ps, Q = c.nc, c.ps, c.Q
    with ExitStack() as ctx:
        PC = ctx.enter_context(nc.sbuf_tensor("cmp_probs", [P, ST, 512], F32))
        ST_ = ctx.enter_context(nc.sbuf_tensor("cmp_stats", [P, 4, ST * NHEAD], F32))
        MASK = ctx.enter_context(nc.sbuf_tensor("cmp_mask", [P, ST, CPAD], F32))
        BIAS = ctx.enter_context(nc.sbuf_tensor("cmp_bias", [P, 2, 512], F32))
        bias_in, mask_in = c.sem("cmp_bias_landed"), c.sem("cmp_mask_landed")
        bias_used = c.sem("cmp_bias_used")
        s_ready, to_exp, exped = c.sem("cmp_scores_ready"), c.sem("cmp_shifted"), c.sem("cmp_exped")
        p_ready, t_ready = c.sem("cmp_probs_ready"), c.sem("cmp_turned")
        heads = PC[:, :, :].rearrange("p i (h n) -> p (i h) n", n=CPAD)
        with nc.Block(no_gpsimd_drain=True) as block:

            @block.sync
            def _(sp):
                sp.dma_start(MASK[:, :, :], c.ios["cmp_mask"]).then_inc(mask_in, 16)
                for i in range(ST):
                    if i >= 2:
                        sp.wait_ge(bias_used, i - 1)
                    sp.dma_start(BIAS[:, i % 2, :], c.ios["cmp_bias"][:, i, :]).then_inc(bias_in, 16)
                    sp.wait_ge(bias_in, 16 * (i + 1))

            @block.tensor
            def _(pe):
                for i in range(ST):
                    for g in (0, 2, 1, 3):
                        rows = slice(64 * (g % 2), 64 * (g % 2) + 64)
                        for r in range(4):
                            at = (r * NGRP + g) * CPAD
                            last = nc.tensor.matmul(ps[:, i + 4 * (g % 2), at:at + CPAD],
                                                    Q[rows, 4 * (g // 2) + r, i * P:(i + 1) * P],
                                                    c.KCC[rows, (g // 2) * CPAD:(g // 2 + 1) * CPAD],
                                                    start=True, stop=True)
                    last.then_inc(s_ready, 1)
                pe.wait_ge(p_ready, 1)
                for r in range(4):
                    for i in range(ST):
                        last = nc.tensor.transpose(ps[:, 4 + r, i * P:(i + 1) * P], PC[:, i, r * P:(r + 1) * P],
                                                   c.ident[:, :])
                    last.then_inc(t_ready, 1)

            @block.vector
            def _(dve):
                v = nc.vector
                mx, tot, inv, sc = (ST_[:, n, :] for n in range(4))
                for i in range(ST):
                    dve.wait_ge(s_ready, i + 1)
                    dve.wait_ge(bias_in, 16 * (i + 1))
                    for h in range(2):
                        out, bias, score = (x.rearrange("p (a b n) -> p b a n", b=2, n=CPAD)[:, h] for x in
                                            (PC[:, i, :], BIAS[:, i % 2, :], ps[:, i + 4 * h, :]))
                        last = v.tensor_tensor(out, score, bias, ALU.add)
                    last.then_inc(bias_used, 1)
                dve.drain()
                v.tensor_reduce(mx, heads, AX, ALU.max)
                dve.drain()
                v.tensor_tensor(heads, heads, mx.unsqueeze(2).broadcast_to([P, ST * NHEAD, CPAD]), ALU.subtract)\
                    .then_inc(to_exp, 1)
                dve.wait_ge(exped, 1)
                dve.wait_ge(mask_in, 16)
                for i in range(ST):
                    ph = PC[:, i, :].rearrange("p (h n) -> p h n", n=CPAD)
                    v.tensor_tensor(ph, ph, MASK[:, i, :].unsqueeze(1).broadcast_to([P, NHEAD, CPAD]), ALU.mult)
                dve.drain()
                v.tensor_reduce(tot, heads, AX, ALU.add)
                dve.drain()
                v.tensor_scalar(tot, tot, 1e-30, None, ALU.max)
                dve.drain()
                v.reciprocal(inv, tot)
                dve.drain()
                v.tensor_tensor(sc.rearrange("p (i h) -> p i h", i=ST), inv.rearrange("p (i h) -> p i h", i=ST),
                                c.G[:, :, 0:NHEAD], ALU.mult)
                dve.drain()
                v.tensor_tensor(heads, heads, sc.unsqueeze(2).broadcast_to([P, ST * NHEAD, CPAD]), ALU.mult)\
                    .then_inc(p_ready, 1)
                for r in range(4):
                    dve.wait_ge(t_ready, r + 1)
                    v.tensor_copy(c.PCT[:, r, :], ps[:, 4 + r, :])

            @block.scalar
            def _(act):
                act.wait_ge(to_exp, 1)
                nc.scalar.activation(heads, heads, ACT.Exp).then_inc(exped, 1)


def causal_attention(c):
    nc, ps, Q, KK = c.nc, c.ps, c.Q, c.KK
    with ExitStack() as ctx:
        def sb(name, shape):
            return ctx.enter_context(nc.sbuf_tensor(name, shape, F32))

        DIST = sb("causal_dist", [P, S])
        QS = sb("queries_now", [P, S])
        CS = sb("cmp_probs_now", [P, S])
        PR = sb("causal_probs", [P, 2, NCAUSAL])
        PT = sb("causal_probs_turned", [P, NCAUSAL])
        MX, RS, SC = sb("causal_max", [P, 2, 4]), sb("causal_sum", [P, 2, 4]), sb("causal_scale", [P, 2, 2, 4])
        dist_in = c.sem("causal_dist_landed")
        by_tile = q_ready, o_read = [c.sig(f"attn_{n}") for n in ("q_ready", "o_read")]
        by_unit = s_ready, s_read, m_ready, e_ready, sc_ready, p_ready, t_ready, t_read, pv_done = [
            c.sig(f"attn_{n}") for n in ("s_ready", "s_read", "max_ready", "exp_ready", "scale_ready",
                                         "p_ready", "turned_ready", "turned_read", "pv_done")]
        prime(c, by_tile + by_unit)
        SB = ps[:, 0:3, :].rearrange("p a n -> p (a n)")
        TB = ps[:, 3:6, :].rearrange("p a n -> p (a n)")
        O = ps[:, 6, :]
        UNITS = 4
        with nc.Block(no_gpsimd_drain=True) as block:

            @block.sync
            def _(sp):
                sp.dma_start(DIST[:, :], c.ios["causal_dist"]).then_inc(dist_in, 16)

            @block.tensor
            def _(pe):
                for half in range(2):
                    with pe.Fori(0, 4) as r:
                        tile0, unit0 = r + 4 * half, r * UNITS + 16 * half
                        for step in range(UNITS + 2):
                            if step < UNITS:
                                p, br = step // 2, step % 2
                                rows = slice(64 * p, 64 * p + 64)
                                if step == 0:
                                    q_ready.wait(pe, tile0 + 1)
                                s_read.wait(pe, unit0 + step)
                                for i, at, n in CAUSAL:
                                    last = nc.tensor.matmul(SB[:, at:at + n], QS[rows, i * P:(i + 1) * P],
                                                            KK[rows, 2 * br + half, 0:n], start=True, stop=True)
                                last.then_inc(s_ready.sem, 1)
                            if 1 <= step <= UNITS:
                                u = step - 1
                                p_ready.wait(pe, unit0 + u + 1)
                                t_read.wait(pe, unit0 + u)
                                for j in range(ST):
                                    for i, at, n in CAUSAL:
                                        if i >= j:
                                            to = PT_AT[j] + (i - j) * P
                                            last = nc.tensor.transpose(TB[:, to:to + P],
                                                                       PR[:, u % 2, at + j * P:at + j * P + P],
                                                                       c.ident[:, :])
                                last.then_inc(t_ready.sem, 1)
                            if step >= 2:
                                u = step - 2
                                p, br = u // 2, u % 2
                                g = 2 * half + p
                                out = O[64 * p:64 * p + 64, :]
                                if u == 0:
                                    o_read.wait(pe, tile0)
                                if br == 0:
                                    rows = slice(CPAD * g, CPAD * g + CPAD)
                                    nc.tensor.matmul(out, c.VCC[rows, :],
                                                     CS[rows, :],
                                                     start=True, stop=False, skip_group_check=True)
                                t_read.wait(pe, unit0 + u + 1)
                                for j in range(ST):
                                    last = nc.tensor.matmul(out[:, j * P:], c.Vt(br, j)[:, g * HD:(g + 1) * HD],
                                                            PT[:, PT_AT[j]:PT_AT[j] + S - j * P],
                                                            start=False, stop=(br == 1 and j == ST - 1),
                                                            skip_group_check=True)
                                last.then_inc(pv_done.sem, 1)

            @block.vector
            def _(dve):
                v = nc.vector
                dve.wait_ge(dist_in, 16)
                for half in range(2):
                    with dve.Fori(0, 4) as r:
                        tile0, unit0 = r + 4 * half, r * UNITS + 16 * half
                        pv_done.wait(dve, unit0)
                        v.tensor_copy(CS[:, :], c.PCT[:, bass.ds(r, 1), :].rearrange("p a n -> p (a n)"))
                        v.tensor_copy(QS[:, :], Q[:, bass.ds(tile0, 1), :].rearrange("p a n -> p (a n)"))\
                            .then_inc(q_ready.sem, 1)
                        for step in range(UNITS + 2):
                            if step < UNITS:
                                p, b = step // 2, step % 2
                                s_ready.wait(dve, unit0 + step + 1)
                                if step >= 2:
                                    t_ready.wait(dve, unit0 + step - 1)
                                for i, at, n in CAUSAL:
                                    last = v.scalar_tensor_tensor(
                                        out=PR[:, b, at:at + n], in0=DIST[:, S - n:],
                                        scalar=c.slopes[:, bass.ds(tile0 * 2 + p, 1)],
                                        in1=SB[:, at:at + n], op0=ALU.mult, op1=ALU.add)
                                last.then_inc(s_read.sem, 1)
                                dve.drain()
                                for i, at, n in CAUSAL:
                                    last = v.tensor_reduce(MX[:, b, i:i + 1], PR[:, b, at:at + n], AX, ALU.max,
                                                           negate=True)
                                last.then_inc(m_ready.sem, 1)
                            if 1 <= step <= UNITS:
                                u = step - 1
                                e_ready.wait(dve, unit0 + u + 1)
                                v.reciprocal(SC[:, u % 2, 0, :], RS[:, u % 2, :])
                                dve.drain()
                                gate = c.G[:, :, bass.ds(tile0 * 2 + (NHEAD * (1 + u % 2) + u // 2), 1)]
                                v.tensor_tensor(SC[:, u % 2, 1, :], SC[:, u % 2, 0, :],
                                                gate.rearrange("p i a -> p (i a)"), ALU.mult).then_inc(sc_ready.sem, 1)
                            if step >= 2:
                                u = step - 2
                                t_ready.wait(dve, unit0 + u + 1)
                                pv_done.wait(dve, unit0 + u)
                                v.tensor_copy(PT[:, :], TB[:, 0:NCAUSAL]).then_inc(t_read.sem, 1)

            @block.scalar
            def _(act):
                for half in range(2):
                    with act.Fori(0, 4) as r:
                        tile0, unit0 = r + 4 * half, r * UNITS + 16 * half
                        for step in range(UNITS + 1):
                            if step < UNITS:
                                b = step % 2
                                m_ready.wait(act, unit0 + step + 1)
                                for i, at, n in CAUSAL:
                                    last = nc.scalar.activation(PR[:, b, at:at + n], PR[:, b, at:at + n], ACT.Exp,
                                                                bias=MX[:, b, i:i + 1], accum_out=RS[:, b, i:i + 1])
                                last.then_inc(e_ready.sem, 1)
                            if step >= 1:
                                u = step - 1
                                sc_ready.wait(act, unit0 + u + 1)
                                for i, at, n in CAUSAL:
                                    last = nc.scalar.activation(PR[:, u % 2, at:at + n], PR[:, u % 2, at:at + n],
                                                                ACT.Copy, scale=SC[:, u % 2, 1, i:i + 1])
                                last.then_inc(p_ready.sem, 1)
                        pv_done.wait(act, unit0 + UNITS)
                        nc.scalar.copy(Q[:, bass.ds(tile0, 1), :].rearrange("p a n -> p (a n)"), O)\
                            .then_inc(o_read.sem, 1)
        for s in by_tile:
            s.passed(KT)
        for s in by_unit:
            s.passed(KT * UNITS)


def mixer_output(c):
    nc, ps, ring, H, Y, Q = c.nc, c.ps, c.ring, c.H, c.Y, c.Q
    with ExitStack() as ctx:
        GA = ctx.enter_context(nc.sbuf_tensor("sigmoid_gm_attn", [P, 2, S], F32))
        z_ready, z_read, y_ready = (c.sig(f"project_{n}").sem for n in ("z_ready", "z_read", "added"))
        with nc.Block(no_gpsimd_drain=True) as block:

            @block.tensor
            def _(pe):
                for u in range(2 * KT):
                    if u % 4 == 0:
                        w = ring.take(pe).rearrange("p (s w) -> p s w", s=4)
                    if u >= 8:
                        pe.wait_ge(z_read, u - 7)
                    if u == KT:
                        pe.wait_ge(y_ready, KT)
                    src = H if u < KT else Y
                    project(nc, ps[:, u % 8, :], w[:, u % 4], lambda k: src[:, k, :]).then_inc(z_ready, 1)
                    if u % 4 == 3:
                        ring.used(z_ready, u + 1)

            @block.scalar
            def _(act):
                for u in range(2 * KT):
                    act.wait_ge(z_ready, u + 1)
                    if u < KT:
                        if u >= 2:
                            act.wait_ge(y_ready, u - 1)
                        nc.scalar.activation(GA[:, u % 2, :], ps[:, u, :], ACT.Sigmoid).then_inc(z_read, 1)
                    else:
                        nc.scalar.copy(H[:, u - KT, :], ps[:, u % 8, :]).then_inc(z_read, 1)

            @block.vector
            def _(dve):
                for u in range(KT):
                    dve.wait_ge(z_read, u + 1)
                    nc.vector.tensor_tensor(Q[:, u, :], Q[:, u, :], GA[:, u % 2, :], ALU.mult)
                    dve.drain()
                    nc.vector.tensor_tensor(Y[:, u, :], Y[:, u, :], Q[:, u, :], ALU.add).then_inc(y_ready, 1)

            @block.sync
            def _(sp):
                ring.feed(sp, ring.uses + Ring.SLOTS)
        c.sig("project_z_ready").passed(2 * KT)
        c.sig("project_z_read").passed(2 * KT)
        c.sig("project_added").passed(KT)


def feed_forward(c, out):
    nc, ps, ring, H = c.nc, c.ps, c.ring, c.H
    with ExitStack() as ctx:
        A = ctx.enter_context(nc.sbuf_tensor("ffn_hidden", [P, FT, S], F32))
        z_ready, silu_ready, a_ready = c.sem("ffn_z_ready"), c.sem("ffn_silu_ready"), c.sem("ffn_hidden_ready")
        o_ready = c.sem("ffn_out_ready")
        with nc.Block(no_gpsimd_drain=True) as block:

            @block.tensor
            def _(pe):
                for j in range(FT):
                    if j % 2 == 0:
                        w = ring.take(pe).rearrange("p (s w) -> p s w", s=4)
                    for s in range(2):
                        if j >= 3:
                            pe.wait_ge(a_ready, j - 2)
                        project(nc, ps[:, 2 * (j % 3) + s, :], w[:, 2 * (j % 2) + s], lambda k: H[:, k, :])\
                            .then_inc(z_ready, 1)
                    if j % 2:
                        ring.used(z_ready, 2 * j + 2)
                for j in range(KT):
                    w = ring.take(pe, FT * P)
                    pe.wait_ge(a_ready, FT)
                    if j >= 2:
                        pe.wait_ge(c.out_read, j - 1)
                    project(nc, ps[:, 6 + j % 2, :], w, lambda k: A[:, k, :], FT).then_inc(o_ready, 1)
                    ring.used(o_ready, j + 1)

            @block.scalar
            def _(act):
                for j in range(FT):
                    act.wait_ge(z_ready, 2 * j + 1)
                    nc.scalar.activation(A[:, j, :], ps[:, 2 * (j % 3), :], ACT.Silu).then_inc(silu_ready, 1)
                for j in range(KT):
                    act.wait_ge(o_ready, j + 1)
                    nc.scalar.copy(out[:, j, :], ps[:, 6 + j % 2, :]).then_inc(c.out_read, 1)

            @block.vector
            def _(dve):
                for j in range(FT):
                    dve.wait_ge(silu_ready, j + 1)
                    dve.wait_ge(z_ready, 2 * j + 2)
                    nc.vector.tensor_tensor(A[:, j, :], A[:, j, :], ps[:, 2 * (j % 3) + 1, :], ALU.mult)\
                        .then_inc(a_ready, 1)

            @block.sync
            def _(sp):
                ring.feed(sp, ring.uses + Ring.SLOTS)


def per_layer_embedding(c):
    nc, ps, ring, X = c.nc, c.ps, c.ring, c.X
    with ExitStack() as ctx:
        PT_ = ctx.enter_context(nc.sbuf_tensor("ple_p", [P, 2, S], F32))
        SG = ctx.enter_context(nc.sbuf_tensor("ple_gate", [P, KT, S], F32))
        p_in, z_ready, s_ready, t_ready = (c.sem("ple_p_landed"), c.sem("ple_z_ready"), c.sem("ple_gate_ready"),
                                           c.sem("ple_proj_ready"))
        added = c.sem("ple_scaled")
        with nc.Block(no_gpsimd_drain=True) as block:

            @block.tensor
            def _(pe):
                for j in range(KT):
                    if j % 4 == 0:
                        w = ring.take(pe).rearrange("p (s w) -> p s w", s=4)
                    if j >= 4:
                        pe.wait_ge(s_ready, j - 3)
                    project(nc, ps[:, j % 4, :], w[:, j % 4], lambda k: X[:, k, 0:S]).then_inc(z_ready, 1)
                    if j % 4 == 3:
                        ring.used(z_ready, j + 1)
                w = ring.take(pe, 2 * D).rearrange("p (s w) -> p s w", s=KT)
                pe.wait_ge(p_in, 16)
                for j in range(KT):
                    if j >= 4:
                        pe.wait_ge(added, j - 3)
                    project(nc, ps[:, 4 + j % 4, :], w[:, j], lambda k: PT_[:, k, :], 2).then_inc(t_ready, 1)
                ring.used(t_ready, KT)

            @block.scalar
            def _(act):
                for j in range(KT):
                    act.wait_ge(z_ready, j + 1)
                    nc.scalar.activation(SG[:, j, :], ps[:, j % 4, :], ACT.Sigmoid, bias=c.vec("ple_b", j))\
                        .then_inc(s_ready, 1)

            @block.vector
            def _(dve):
                dve.wait_ge(s_ready, KT)
                for j in range(KT):
                    dve.wait_ge(t_ready, j + 1)
                    nc.vector.tensor_tensor(SG[:, j, :], SG[:, j, :], ps[:, 4 + j % 4, :], ALU.mult)\
                        .then_inc(added, 1)
                    dve.drain()
                    nc.vector.tensor_tensor(X[:, j, 0:S], X[:, j, 0:S], SG[:, j, :], ALU.add)

            @block.sync
            def _(sp):
                sp.dma_start(PT_[:, :, :], c.ios["pT"].rearrange("(k p) t -> p k t", p=P)).then_inc(p_in, 16)
                ring.feed(sp, ring.uses + Ring.SLOTS)



NPIECE = 384
H2_ORDER = [h for t in range(4) for h in (t, 4 + t)]
U_AT = {0: 1, S: S + 2}
UW = T + 3
NOVF = 2 * T // CAP
NBLK = NEXP + NOVF
RW = NEG + NEXP
UNIT_A = ([(1, 128, 640, 0), (2, 768, 640, 384)],
          [(1, 128, 0, 384), (1, 512, S, C), (2, 768, S, C), (2, 1024, 128, 384)])
UNIT_B = ([(0, 0, 512, 128), (3, 512, 512, 384)],
          [(0, 0, 0, 256), (0, 256, S, C), (3, 512, S, C), (3, 768, 256, 256)])
UNIT_C = ([(4, 0, 256, 384), (5, 256, 256, 384)], [(4, 0, S, C), (5, 256, S, C)])


def second_chunks(ios):
    out = [ios["w_ada"][4 * j:4 * j + 4].rearrange("t p w -> p t w") for j in range(NL * 12)]
    for l in range(NL):
        def tiles(name, at, n, per):
            return ios[name][per * l + at:per * l + at + n].rearrange("t p w -> p t w")
        out += [tiles("w_in2", 0, 4, 13), tiles("w_in2", 4, 4, 13), tiles("w_in2", 8, 4, 13), tiles("w_in2", 12, 1, 13)]
        out += [ios["w_nat2"][l].rearrange("(k p) n -> p k n", p=P)]
        out += [tiles("w_out2", 0, 4, KT), tiles("w_out2", 4, 4, KT)]
        for e in range(NEXP):
            out += expert_chunks(ios, l, e)
    return out


def expert_chunks(ios, l, e):
    at = slice(l * NEXP + e, l * NEXP + e + 1) if isinstance(e, int) else bass.ds(e + l * NEXP, 1)
    up = [ios[n][at].rearrange("e (p k) n -> p (e k) n", k=KT) for n in ("w1", "w3")]
    return up + [ios["w2"][at].rearrange("e (j p) n -> p (e j) n", p=P)]


def second_setup(c):
    c.signals = {}

    def sig(name):
        if name not in c.signals:
            c.signals[name] = Signal(c.sem(name))
        return c.signals[name]
    c.sig = sig
    nc = c.nc
    c.tokens = nc.dram_tensor("token_rows", (T, D), F32, kind="Internal").ap()
    c.slot_token = nc.dram_tensor("slot_tokens", (NBLK * CAP, 1), F32, kind="Internal").ap()
    c.expert_out = nc.dram_tensor("expert_rows", (NBLK * CAP, D), F32, kind="Internal").ap()


def modulations(c):
    nc, ps, ring = c.nc, c.ps, c.ring
    with ExitStack() as ctx:
        CA = ctx.enter_context(nc.sbuf_tensor("conditions", [P, KT, 2], F32))
        BA = ctx.enter_context(nc.sbuf_tensor("ada_bias", [P, NL * 48], F32))
        cond_in, silu, done = c.sem("conditions_landed"), c.sem("conditions_silu"), c.sem("mod_ready")
        x_in = c.sem("context_landed")
        with nc.Block(no_gpsimd_drain=True) as block:

            @block.tensor
            def _(pe):
                pe.wait_ge(silu, 1)
                for f in range(NL * 48):
                    if f % 4 == 0:
                        w = ring.take(pe).rearrange("p (s w) -> p s w", s=4)
                    last = project(nc, ps[:, f // 48, 2 * (f % 48):2 * (f % 48) + 2], w[:, f % 4],
                                   lambda k: CA[:, k, :])
                    if f % 4 == 3:
                        last.then_inc(done, 1)
                        ring.used(done, f // 4 + 1)

            @block.sync
            def _(sp):
                sp.dma_start(CA[:, :, :], c.ios["cond"]).then_inc(cond_in, 16)
                sp.dma_start(BA[:, :], c.ios["b_ada"]).then_inc(cond_in, 16)
                sp.dma_start(c.expert_out[NEXP * CAP:, :], c.ios["zeros"].partition_broadcast(NOVF * CAP))\
                    .then_inc(x_in, 16)
                sp.dma_start(c.X[:, :, S:T], c.ios["ctxT"].rearrange("(k p) t -> p k t", p=P)).then_inc(x_in, 16)
                ring.feed(sp, ring.uses + Ring.SLOTS)
                sp.wait_ge(x_in, 32)

            @block.scalar
            def _(act):
                act.wait_ge(cond_in, 32)
                nc.scalar.activation(CA[:, :, :], CA[:, :, :], ACT.Silu).then_inc(silu, 1)

            @block.vector
            def _(dve):
                dve.wait_ge(cond_in, 32)
                for l in range(NL):
                    dve.wait_ge(done, 12 * (l + 1))
                    mod = c.mod[:, l, :, :]
                    nc.vector.tensor_tensor(mod, ps[:, l, 0:96].rearrange("p (f v) -> p f v", v=2),
                                            BA[:, l * 48:(l + 1) * 48].unsqueeze(2).broadcast_to([P, 48, 2]), ALU.add)
                    dve.drain()
                    for n in (1, 4):
                        scales = c.mod[:, l, 8 * n:8 * n + 8, :]
                        nc.vector.tensor_scalar(scales, scales, 1.0, None, ALU.add)


def modulate(c, l, n, HX, parts):
    nc = c.nc
    with nc.Block(no_gpsimd_drain=True) as block:

        @block.vector
        def _(dve):
            for k in range(KT):
                for v, (at, width) in enumerate(parts):
                    nc.vector.tensor_scalar(HX[:, k, at:at + width], c.X[:, k, at:at + width],
                                            c.mod[:, l, 8 * (n + 1) + k, v:v + 1], c.mod[:, l, 8 * n + k, v:v + 1],
                                            ALU.mult, ALU.add)


def mixer_inputs(c, l, HX, MIX, K, VG, parts):
    nc, ps, ring = c.nc, c.ps, c.ring
    last_layer = l == NL - 1
    whole = [(0, S)] if last_layer else [(0, NPIECE), (NPIECE, NPIECE)]
    ntok = (S if last_layer else T) // P
    with ExitStack() as ctx:
        def sb(name, shape):
            return ctx.enter_context(nc.sbuf_tensor(f"{name}_{l}", shape, F32))

        UP, CX = sb("conv_in", [P, 2, UW]), sb("conv_cx", [P, 2, T])
        COS, SIN, ROT = sb("rope_cos", [P, S]), sb("rope_sin", [P, S]), sb("rope_rot", [P, P])
        WS, BS, CW = sb("gm_w", [P, 4, P]), sb("gm_b", [P, 2, P]), sb("conv2_w", [P, 2, 3])
        BN, MV, RV = sb("gm_bn", [P, TT, 6]), sb("gm_mean_var", [P, TT, 2]), sb("gm_rstd", [P, TT, 2])
        consts, z_ready, z_read = c.sig("mix2_consts_landed"), c.sig("mix2_z_ready"), c.sig("mix2_z_read")
        nat_ready, nat_read = c.sig("mix2_nat_ready"), c.sig("mix2_nat_read")
        rot_ready, rot_read = c.sig("mix2_rot_ready"), c.sig("mix2_rot_read")
        var_ready, root_ready = c.sig("mix2_var_ready"), c.sig("mix2_root_ready")
        v_ready, gm_ready = c.sig("mix2_v_ready"), c.sig("mix2_gm_ready")
        q_read = c.sig("mix2_q_evacuated")

        def place(tile, at, n):
            if tile < 4:
                return [(MIX[:, tile, at:at + n], 0, n)]
            if tile == 4:
                return [(K[:, at:at + n], 0, n)]
            if tile in (5, 6):
                out = []
                for start, end in ((0, S), (S, T)):
                    a, b = max(at, start), min(at + n, end)
                    if a < b:
                        out.append((UP[:, tile - 5, U_AT[start] + a - start:U_AT[start] + b - start], a - at, b - at))
                return out
            if tile in (8, 9):
                return [(CX[:, tile - 8, at:at + n], 0, n)]
            return [(MIX[:, {7: 6, 12: 7, 10: 4, 11: 5}[tile], at:at + n], 0, n)]

        pieces = [(tile, at, n) for tile in range(13)
                  for at, n in (whole + [(S, C)] if tile == 4 and last_layer else whole)]
        nrot = 5
        with nc.Block(no_gpsimd_drain=True) as block:

            @block.tensor
            def _(pe):
                u, chunk_of = 0, None
                for u, (tile, at, n) in enumerate(pieces):
                    if tile // 4 != chunk_of:
                        if chunk_of is not None:
                            ring.used(z_ready.sem, z_ready.base + u)
                        chunk_of = tile // 4
                        w = ring.take(pe, KT * P * (4 if tile < 12 else 1)).rearrange("p (s w) -> p s w", w=KT * P)
                    if u >= 4:
                        z_read.wait(pe, u - 3)
                    project(nc, ps[:, u % 4, 0:n], w[:, tile % 4], lambda k: HX[:, k, at:at + n])\
                        .then_inc(z_ready.sem, 1)
                ring.used(z_ready.sem, z_ready.base + len(pieces))
                w = ring.take(pe, KT * NPIECE).rearrange("p (k n) -> p k n", k=KT)
                for i in range(TT):
                    if i >= 2:
                        nat_read.wait(pe, i - 1)
                    n = NPIECE if i < ntok else P
                    for k in range(KT):
                        last = nc.tensor.matmul(ps[:, 4 + i % 2, 0:n], HX[:, k, i * P:(i + 1) * P], w[:, k, 0:n],
                                                start=(k == 0), stop=(k == KT - 1))
                    last.then_inc(nat_ready.sem, 1)
                ring.used(nat_ready.sem, nat_ready.base + TT)
                consts.wait(pe, 16 * 6)
                for j in range(nrot):
                    if j >= 2:
                        rot_read.wait(pe, j - 1)
                    src = MIX[:, j, 0:S] if j < 4 else K[:, 0:S]
                    nc.tensor.matmul(ps[:, 6 + j % 2, :], ROT[:, :], src, start=True, stop=True)\
                        .then_inc(rot_ready.sem, 1)
                v_ready.wait(pe, 1)
                for h in range(2):
                    for i in range(ntok):
                        for g in (2 * h, 2 * h + 1):
                            bank, at = (h, i * P) if i < ST else (2 + h, (i - ST) * P)
                            last = nc.tensor.matmul(ps[64 * (g % 2):64 * (g % 2) + 64, bank, at:at + P],
                                                    VG[:, i, P + g * 64:P + (g + 1) * 64], WS[:, g, :],
                                                    start=True, stop=True)
                last.then_inc(gm_ready.sem, 1)

            @block.sync
            def _(sp):
                for dst, src in ((COS[:, :], "rope_cos"), (SIN[:, :], "rope_sin"), (ROT[:, :], "rope_rot")):
                    sp.dma_start(dst, c.ios[src]).then_inc(consts.sem, 16)
                sp.dma_start(WS[:, :, :], c.ios["gm_w"][l]).then_inc(consts.sem, 16)
                sp.dma_start(BS[:, :, :], c.ios["gm_b"][l]).then_inc(consts.sem, 16)
                sp.dma_start(CW[:, :, :], c.ios["conv2"][l]).then_inc(consts.sem, 16)
                ring.feed(sp, ring.uses + Ring.SLOTS)

            @block.scalar
            def _(act):
                for u, (tile, at, n) in enumerate(pieces):
                    z_ready.wait(act, u + 1)
                    for dst, a, b in place(tile, at, n):
                        src = ps[:, u % 4, a:b]
                        if tile < 4:
                            last = nc.scalar.mul(dst, src, HD ** -0.5)
                        elif tile in (7, 12):
                            last = nc.scalar.activation(dst, src, ACT.Gelu_apprx_tanh)
                        else:
                            last = nc.scalar.copy(dst, src)
                    last.then_inc(z_read.sem, 1)
                for i in range(TT):
                    nat_ready.wait(act, i + 1)
                    last = nc.scalar.copy(VG[:, i, 0:P], ps[:, 4 + i % 2, 0:P])
                    if i < ntok:
                        last = nc.scalar.activation(VG[:, i, P:], ps[:, 4 + i % 2, P:NPIECE], ACT.Gelu_apprx_tanh)
                    last.then_inc(nat_read.sem, 1)
                var_ready.wait(act, 1)
                nc.scalar.activation(RV[:, 0:ntok, 1], RV[:, 0:ntok, 0], ACT.Sqrt).then_inc(root_ready.sem, 1)

            @block.vector
            def _(dve):
                v = nc.vector
                consts.wait(dve, 16 * 6)
                for at in (0, S + 1, UW - 1):
                    v.memset(UP[:, :, at:at + 1], 0.0)
                z_read.wait(dve, sum(1 for tile, _, _ in pieces if tile < 12))
                for start, width in parts:
                    up = UP[:, :, U_AT[start]:U_AT[start] + width]
                    v.tensor_tensor(up, up, CX[:, :, start:start + width], ALU.mult)
                dve.drain()
                for h in range(2):
                    for start, width in parts:
                        at, acc = U_AT[start], CX[:, h, start:start + width]
                        v.tensor_scalar(acc, UP[:, h, at - 1:at - 1 + width], CW[:, h, 0:1], None, ALU.mult)
                        for t in (1, 2):
                            dve.drain()
                            v.scalar_tensor_tensor(out=acc, in0=UP[:, h, at - 1 + t:at - 1 + t + width],
                                                   scalar=CW[:, h, t:t + 1], in1=acc, op0=ALU.mult, op1=ALU.add)
                        dve.drain()
                        y = MIX[:, 4 + h, start:start + width]
                        v.tensor_tensor(y, y, acc, ALU.mult)
                nat_read.wait(dve, TT)
                for i in range(ntok):
                    v.bn_stats(BN[:, i, :], VG[:, i, P:])
                dve.drain()
                for i in range(ntok):
                    v.bn_aggr(MV[:, i, :], BN[:, i, :])
                dve.drain()
                v.tensor_scalar(MV[:, 0:ntok, 1], MV[:, 0:ntok, 1], EPS, None, ALU.add)
                dve.drain()
                v.reciprocal(RV[:, 0:ntok, 0], MV[:, 0:ntok, 1]).then_inc(var_ready.sem, 1)
                root_ready.wait(dve, 1)
                for i in range(ntok):
                    last = v.tensor_scalar(VG[:, i, P:], VG[:, i, P:], MV[:, i, 0:1], RV[:, i, 1:2],
                                           ALU.subtract, ALU.mult)
                last.then_inc(v_ready.sem, 1)
                for j in range(nrot):
                    x = MIX[:, j, 0:S] if j < 4 else K[:, 0:S]
                    rot_ready.wait(dve, j + 1)
                    v.tensor_tensor(x, x, COS[:, :], ALU.mult)
                    v.tensor_tensor(CX[:, j % 2, 0:S], ps[:, 6 + j % 2, :], SIN[:, :], ALU.mult)\
                        .then_inc(rot_read.sem, 1)
                    dve.drain()
                    v.tensor_tensor(x, x, CX[:, j % 2, 0:S], ALU.add)
                dve.drain()
                gm_ready.wait(dve, 1)
                for h in range(2):
                    for n, (start, width) in enumerate(parts):
                        if start < ntok * P:
                            chunks = width // P
                            s = CX[:, h, start:start + width].rearrange("p (i t) -> p i t", t=P)
                            v.tensor_tensor(s, ps[:, 2 * n + h, 0:width].rearrange("p (i t) -> p i t", t=P),
                                            BS[:, h, :].unsqueeze(1).broadcast_to([P, chunks, P]), ALU.add)
                dve.drain()
                for h in range(2):
                    for start, width in parts:
                        y = MIX[:, 6 + h, start:start + width]
                        v.tensor_tensor(y, y, CX[:, h, start:start + width], ALU.mult)
        consts.passed(16 * 6)
        z_ready.passed(len(pieces))
        z_read.passed(len(pieces))
        nat_ready.passed(TT)
        nat_read.passed(TT)
        rot_ready.passed(nrot)
        rot_read.passed(nrot)
        for s in (var_ready, root_ready, v_ready, gm_ready):
            s.passed(1)


def window_attention(c, l, MIX, K, VG):
    nc, ps = c.nc, c.ps
    units = [UNIT_A, UNIT_B] + ([UNIT_C] if l < NL - 1 else [])
    plan = [(p, segs, prods) for p in range(2) for segs, prods in units]
    width = T if l < NL - 1 else S
    with ExitStack() as ctx:
        def sb(name, shape):
            return ctx.enter_context(nc.sbuf_tensor(f"{name}_{l}", shape, F32))

        QS, MASK, SINK = sb("win_queries", [P, T]), sb("win_mask", [P, 1024]), sb("win_sink", [P, H2])
        PR, PT = sb("win_probs", [P, 2, 1536]), sb("win_turned", [P, 2, NCAUSAL])
        MX, NM, RS, ES, SC = (sb(f"win_{n}", [P, 2, 2]) for n in ("max", "negmax", "sum", "sink_exp", "scale"))
        consts = c.sig("win_consts_landed")
        q_ready, s_ready, s_read = c.sig("attn_q_ready"), c.sig("attn_s_ready"), c.sig("attn_s_read")
        m_ready, e_ready, sc_ready = c.sig("attn_max_ready"), c.sig("attn_exp_ready"), c.sig("attn_scale_ready")
        p_ready, t_ready, t_read = c.sig("attn_p_ready"), c.sig("attn_turned_ready"), c.sig("attn_turned_read")
        pv_done, o_read = c.sig("attn_pv_done"), c.sig("attn_o_read")
        SB = ps[:, 0:3, :].rearrange("p a n -> p (a n)")
        TB = ps[:, 3:6, :].rearrange("p a n -> p (a n)")
        N = len(plan)

        def blocks(segs, prods):
            return [(i, at + b * P, (key + b * P) // P) for i, at, key, n in prods for b in range(n // P)]

        with nc.Block(no_gpsimd_drain=True) as block:

            @block.sync
            def _(sp):
                sp.dma_start(MASK[:, :], c.ios["win_mask"]).then_inc(consts.sem, 16)
                sp.dma_start(SINK[:, :], c.ios["sink"][l]).then_inc(consts.sem, 16)

            @block.tensor
            def _(pe):
                with pe.Fori(0, 4) as t:
                    for step in range(N + 2):
                        if step < N:
                            p, segs, prods = plan[step]
                            rows = slice(64 * p, 64 * p + 64)
                            if step == 0:
                                q_ready.wait(pe, t + 1)
                            s_read.wait(pe, t * N + step)
                            for i, at, key, n in prods:
                                last = nc.tensor.matmul(SB[:, at:at + n], QS[rows, i * P:(i + 1) * P],
                                                        K[rows, key:key + n], start=True, stop=True)
                            last.then_inc(s_ready.sem, 1)
                        if 1 <= step <= N:
                            u = step - 1
                            p_ready.wait(pe, t * N + u + 1)
                            t_read.wait(pe, t * N + u)
                            for n, (i, at, key) in enumerate(blocks(*plan[u][1:])):
                                last = nc.tensor.transpose(TB[:, n * P:(n + 1) * P], PR[:, u % 2, at:at + P],
                                                           c.ident[:, :])
                            last.then_inc(t_ready.sem, 1)
                        if step >= 2:
                            u = step - 2
                            p, segs, prods = plan[u]
                            if u == 0:
                                o_read.wait(pe, t)
                            t_read.wait(pe, t * N + u + 1)
                            bl = blocks(segs, prods)
                            for i in sorted({b[0] for b in bl}):
                                mine = [(n, b[2]) for n, b in enumerate(bl) if b[0] == i]
                                out = ps[64 * p:64 * p + 64, 6 + i // ST, (i % ST) * P:(i % ST + 1) * P]
                                for m, (n, key) in enumerate(mine):
                                    last = nc.tensor.matmul(out, VG[:, key, 64 * p:64 * p + 64],
                                                            PT[:, u % 2, n * P:(n + 1) * P],
                                                            start=(m == 0), stop=(m == len(mine) - 1))
                            last.then_inc(pv_done.sem, 1)

            @block.vector
            def _(dve):
                v = nc.vector
                consts.wait(dve, 32)
                with dve.Fori(0, 4) as t:
                    s_ready.wait(dve, t * N)
                    v.tensor_copy(QS[:, 0:width], MIX[:, bass.ds(t, 1), 0:width].rearrange("p a n -> p (a n)"))\
                        .then_inc(q_ready.sem, 1)
                    for step in range(N + 2):
                        if step < N:
                            p, segs, _ = plan[step]
                            b = step % 2
                            s_ready.wait(dve, t * N + step + 1)
                            if step >= 2:
                                t_ready.wait(dve, t * N + step - 1)
                            for n, (i, at, w, m) in enumerate(segs):
                                last = v.scalar_tensor_tensor(out=PR[:, b, at:at + w], in0=SB[:, at:at + w], scalar=1.0,
                                                              in1=MASK[:, m:m + w], op0=ALU.mult, op1=ALU.add)
                            last.then_inc(s_read.sem, 1)
                            dve.drain()
                            for n, (i, at, w, m) in enumerate(segs):
                                v.tensor_reduce(MX[:, b, n:n + 1], PR[:, b, at:at + w], AX, ALU.max)
                            dve.drain()
                            v.tensor_scalar(NM[:, b, :], MX[:, b, :], SINK[:, bass.ds(t * 2 + p, 1)], -1.0,
                                            ALU.max, ALU.mult).then_inc(m_ready.sem, 1)
                        if 1 <= step <= N:
                            u = step - 1
                            b = u % 2
                            e_ready.wait(dve, t * N + u + 1)
                            v.tensor_tensor(RS[:, b, :], RS[:, b, :], ES[:, b, :], ALU.add)
                            dve.drain()
                            v.reciprocal(SC[:, b, :], RS[:, b, :]).then_inc(sc_ready.sem, 1)
                        if step >= 2:
                            u = step - 2
                            n = len(blocks(*plan[u][1:])) * P
                            t_ready.wait(dve, t * N + u + 1)
                            if u >= 2:
                                pv_done.wait(dve, t * N + u - 1)
                            v.tensor_copy(PT[:, u % 2, 0:n], TB[:, 0:n]).then_inc(t_read.sem, 1)

            @block.scalar
            def _(act):
                consts.wait(act, 32)
                with act.Fori(0, 4) as t:
                    for step in range(N + 1):
                        if step < N:
                            p, segs, _ = plan[step]
                            b = step % 2
                            m_ready.wait(act, t * N + step + 1)
                            for n, (i, at, w, m) in enumerate(segs):
                                nc.scalar.activation(PR[:, b, at:at + w], PR[:, b, at:at + w], ACT.Exp,
                                                     bias=NM[:, b, n:n + 1], accum_out=RS[:, b, n:n + 1])
                                last = nc.scalar.activation(ES[:, b, n:n + 1], SINK[:, bass.ds(t * 2 + p, 1)], ACT.Exp,
                                                            bias=NM[:, b, n:n + 1])
                            last.then_inc(e_ready.sem, 1)
                        if step >= 1:
                            u = step - 1
                            sc_ready.wait(act, t * N + u + 1)
                            for n, (i, at, w, m) in enumerate(plan[u][1]):
                                last = nc.scalar.activation(PR[:, u % 2, at:at + w], PR[:, u % 2, at:at + w],
                                                            ACT.Copy, scale=SC[:, u % 2, n:n + 1])
                            last.then_inc(p_ready.sem, 1)
                    pv_done.wait(act, t * N + N)
                    out = MIX[:, bass.ds(t, 1), 0:width].rearrange("p a n -> p (a n)")
                    last = nc.scalar.copy(out[:, 0:S], ps[:, 6, :])
                    if width > S:
                        last = nc.scalar.copy(out[:, S:T], ps[:, 7, 0:C])
                    last.then_inc(o_read.sem, 1)
        consts.passed(32)
        q_ready.passed(4)
        o_read.passed(4)
        for s in (s_ready, s_read, m_ready, e_ready, sc_ready, p_ready, t_ready, t_read, pv_done):
            s.passed(4 * N)


def mixer_project(c, l, MIX, parts):
    nc, ps, ring = c.nc, c.ps, c.ring
    with ExitStack() as ctx:
        Z = ctx.enter_context(nc.sbuf_tensor(f"mix2_out_{l}", [P, 4, S], F32))
        z_ready, z_read, added = c.sig("project_z_ready"), c.sig("project_z_read"), c.sig("project_added")
        pieces = [(k, v, at, n) for k in range(KT) for v, (at, n) in enumerate(parts)]
        with nc.Block(no_gpsimd_drain=True) as block:

            @block.tensor
            def _(pe):
                for u, (tile, v, at, n) in enumerate(pieces):
                    if tile % 4 == 0 and v == 0:
                        w = ring.take(pe).rearrange("p (s w) -> p s w", s=4)
                    if u >= 8:
                        z_read.wait(pe, u - 7)
                    project(nc, ps[:, u % 8, 0:n], w[:, tile % 4], lambda k: MIX[:, k, at:at + n])\
                        .then_inc(z_ready.sem, 1)
                    if tile % 4 == 3 and v == len(parts) - 1:
                        ring.used(z_ready.sem, z_ready.base + u + 1)

            @block.scalar
            def _(act):
                for u, (tile, v, at, n) in enumerate(pieces):
                    z_ready.wait(act, u + 1)
                    if u >= 4:
                        added.wait(act, u - 3)
                    nc.scalar.activation(Z[:, u % 4, 0:n], ps[:, u % 8, 0:n], ACT.Copy,
                                         scale=c.mod[:, l, 16 + tile, v:v + 1]).then_inc(z_read.sem, 1)

            @block.vector
            def _(dve):
                for u, (tile, v, at, n) in enumerate(pieces):
                    z_read.wait(dve, u + 1)
                    x = c.X[:, tile, at:at + n]
                    nc.vector.scalar_tensor_tensor(out=x, in0=x, scalar=ALPHA, in1=Z[:, u % 4, 0:n],
                                                   op0=ALU.mult, op1=ALU.add).then_inc(added.sem, 1)

            @block.sync
            def _(sp):
                ring.feed(sp, ring.uses + Ring.SLOTS)
        for s in (z_ready, z_read, added):
            s.passed(len(pieces))


def layer_norm(c, n, gain, bias):
    nc, ps, X, ph = c.nc, c.ps, c.X, c.ph
    with stat_buffers(c), ExitStack() as ctx:
        sq = ctx.enter_context(nc.sbuf_tensor(f"squares{c.stat_count}", [P, KT, T], F32))
        banks = [(b, at, min(512, n - at)) for b, at in enumerate(range(0, n, 512))]
        with nc.Block(no_gpsimd_drain=True) as block:

            @block.vector
            def _(dve):
                v = nc.vector
                v.tensor_reduce(c.stat[:, 0:n], X[:, :, 0:n].rearrange("p k t -> p t k"), AX, ALU.add)\
                    .then_inc(ph[0].sem, 1)
                ph[1].wait(dve, 1)
                for b, at, w in banks:
                    x = X[:, :, at:at + w]
                    v.tensor_tensor(x, x, ps[:, b, 0:w].unsqueeze(1).broadcast_to([P, KT, w]), ALU.subtract)

            @block.tensor
            def _(pe):
                ph[0].wait(pe, 1)
                for b, at, w in banks:
                    last = nc.tensor.matmul(ps[:, b, 0:w], c.mean_w[:, :], c.stat[:, at:at + w], start=True, stop=True)
                last.then_inc(ph[1].sem, 1)
        ph[0].passed(1)
        ph[1].passed(1)
        rms_scale(c, X[:, :, 0:n], sq, n)
        with nc.Block(no_gpsimd_drain=True) as block:

            @block.vector
            def _(dve):
                for k in range(KT):
                    nc.vector.scalar_tensor_tensor(out=X[:, k, 0:n], in0=X[:, k, 0:n], scalar=c.vec(gain, k),
                                                   in1=c.rstd[:, 0:n], op0=ALU.mult, op1=ALU.mult)\
                        .then_inc(ph[0].sem, 1)

            @block.scalar
            def _(act):
                for k in range(KT):
                    ph[0].wait(act, k + 1)
                    nc.scalar.activation(X[:, k, 0:n], X[:, k, 0:n], ACT.Identity, bias=c.vec(bias, k))
        ph[0].passed(KT)


def route(c, l, HX, R, nt):
    nc, ps = c.nc, c.ps
    with ExitStack() as ctx:
        def sb(name, shape, dt=F32):
            return ctx.enter_context(nc.sbuf_tensor(f"{name}_{l}", shape, dt))

        WR, BR = sb("router_w", [P, KT, RW]), sb("router_b", [P, RW])
        TRI, ONES, K32 = sb("earlier_tokens", [P, P]), sb("all_tokens", [P, P]), sb("router_consts", [P, 96])
        ROW = sb("token_row", [P, 2, D])
        LG, EM, EQ = sb("logits", [P, TT, RW]), sb("expert_logits", [P, TT, NEXP]), sb("equal", [P, TT, NEXP])
        OH, OHS, SCR = sb("one_hots", [P, 2, TT, NEXP]), sb("one_hot_sum", [P, TT, NEXP]), sb("scratch", [P, TT, NEXP])
        OG, GE, MG = sb("group_one_hot", [P, TT, NEG]), sb("group_exp", [P, TT, NEG]), sb("group_mask", [P, TT, NEG])
        V1 = sb("router_small", [P, 12, 2, TT])
        CB = sb("count_blocks", [P, NEXP, 8])
        CE = sb("expert_counts", [P, 4, NEXP])
        JB = sb("block_of_slot", [P, 2 * TT, 8])
        OB = sb("overflow_experts", [P, NOVF, NEXP])
        IDS, TAB, ZT = sb("token_ids", [P, TT]), sb("slot_table", [NBLK, CAP]), sb("zero_table", [NBLK, CAP])
        consts, row_ready, row_out = c.sig("route_consts_landed"), c.sig("route_row_turned"), c.sig("route_row_copied")
        stored, logit_ready = c.sig("route_rows_stored"), c.sig("route_logits_ready")
        to_exp, exped, gate_exp = c.sig("route_exp_wanted"), c.sig("route_exped"), c.sig("route_gates_ready")
        oh_ready, rank_ready = c.sig("route_one_hots_ready"), c.sig("route_ranks_ready")
        slots_ready, zeroed = c.sig("route_slots_ready"), c.sig("route_table_zeroed")
        scattered, tab_in = c.sig("route_table_scattered"), c.sig("route_table_landed")
        tab_turned, zt = c.sig("route_table_turned"), c.sig("route_zeros_ready")
        desc32, idx32, caps, bidx = K32[:, 0:32], K32[:, 32:64], K32[:, 64:72], K32[:, 72:72 + NOVF]
        with nc.Block() as block:

            @block.sync
            def _(sp):
                for dst, src in ((WR[:, :, :], c.ios["w_router"][l].rearrange("(k p) n -> p k n", p=P)),
                                 (BR[:, :], c.ios["b_router"][l]), (TRI[:, :], c.ios["earlier"]),
                                 (K32[:, :], c.ios["router_consts"]), (IDS[:, :], c.ios["token_ids"])):
                    sp.dma_start(dst, src).then_inc(consts.sem, 16)
                zt.wait(sp, 1)
                sp.dma_start(c.slot_token.rearrange("(b s) o -> b (s o)", s=CAP), ZT[:, :]).then_inc(zeroed.sem, 16)
                for i in range(nt):
                    row_out.wait(sp, 2 * i + 2)
                    sp.dma_start(c.tokens[i * P:(i + 1) * P, :], ROW[:, i % 2, :]).then_inc(stored.sem, 16)
                    stored.wait(sp, 16 * (i + 1))
                scattered.wait(sp, 16 * 2 * nt)
                sp.dma_start(TAB[:, :], c.slot_token.rearrange("(b s) o -> b (s o)", s=CAP)).then_inc(tab_in.sem, 16)

            @block.tensor
            def _(pe):
                consts.wait(pe, 16 * 5)
                for i in range(nt):
                    for k in range(KT):
                        last = nc.tensor.matmul(ps[:, 6, i * RW:(i + 1) * RW], HX[:, k, i * P:(i + 1) * P], WR[:, k, :],
                                                start=(k == 0), stop=(k == KT - 1))
                last.then_inc(logit_ready.sem, 1)
                for i in range(nt):
                    for h in range(2):
                        u = 2 * i + h
                        if u >= 4:
                            row_out.wait(pe, u - 3)
                        for k in range(4):
                            last = nc.tensor.transpose(ps[:, u % 4, k * P:(k + 1) * P],
                                                       HX[:, 4 * h + k, i * P:(i + 1) * P], c.ident[:, :])
                        last.then_inc(row_ready.sem, 1)
                oh_ready.wait(pe, 1)
                for i in range(nt):
                    for m in range(i + 1):
                        nc.tensor.matmul(ps[:, 4, i * NEXP:(i + 1) * NEXP], TRI[:, :] if m == i else ONES[:, :],
                                         OHS[:, m, :], start=(m == 0), stop=(m == i))
                for m in range(nt):
                    last = nc.tensor.matmul(ps[:, 4, 256:256 + NEXP], ONES[:, :], OHS[:, m, :],
                                            start=(m == 0), stop=(m == nt - 1))
                last.then_inc(rank_ready.sem, 1)
                tab_in.wait(pe, 16)
                nc.tensor.transpose(ps[0:CAP, 5, 0:NBLK], TAB[:, :], c.ident[0:NBLK, 0:NBLK]).then_inc(tab_turned.sem, 1)

            @block.scalar
            def _(act):
                for i in range(nt):
                    if i >= 2:
                        stored.wait(act, 16 * (i - 1))
                    for h in range(2):
                        row_ready.wait(act, 2 * i + h + 1)
                        nc.scalar.copy(ROW[:, i % 2, 512 * h:512 * (h + 1)], ps[:, (2 * i + h) % 4, :])\
                            .then_inc(row_out.sem, 1)
                to_exp.wait(act, 1)
                nc.scalar.activation(GE[:, 0:nt, :], GE[:, 0:nt, :], ACT.Exp)
                nc.scalar.activation(V1[:, 3, 0, 0:nt], V1[:, 2, 0, 0:nt], ACT.Exp).then_inc(exped.sem, 1)

            @block.gpsimd
            def _(pool):
                slots_ready.wait(pool, 1)
                zeroed.wait(pool, 16)
                consts.wait(pool, 16 * 5)
                for k in range(2):
                    for i in range(nt):
                        pool.indirect_dma_start(c.slot_token, bass.IndirectOffsetOnAxis(R.slot[:, k, i:i + 1], 0),
                                                IDS[:, i:i + 1], None).then_inc(scattered.sem, 16)

            @block.vector
            def _(dve):
                v = nc.vector
                n3 = lambda x, w: x.unsqueeze(2).broadcast_to([P, nt, w])
                row = lambda x, w: x.unsqueeze(1).broadcast_to([P, nt, w])
                v.memset(ONES[:, :], 1.0)
                v.memset(ZT[:, :], 0.0).then_inc(zt.sem, 1)
                consts.wait(dve, 16 * 5)
                logit_ready.wait(dve, 1)
                lg, em, eq, scr = LG[:, 0:nt, :], EM[:, 0:nt, :], EQ[:, 0:nt, :], SCR[:, 0:nt, :]
                og, ge, mg = OG[:, 0:nt, :], GE[:, 0:nt, :], MG[:, 0:nt, :]
                gl, el = lg[:, :, 0:NEG], lg[:, :, NEG:RW]
                small = lambda n, k=0: V1[:, n, k, 0:nt]
                v.tensor_tensor(lg, ps[:, 6, 0:nt * RW].rearrange("p (i n) -> p i n", n=RW), row(BR[:, :], RW), ALU.add)
                dve.drain()

                def first_of(out, x, best, w, scratch, top):
                    v.tensor_tensor(scratch, x, n3(best, w), ALU.is_equal)
                    dve.drain()
                    v.tensor_tensor(scratch, scratch, row(desc32[:, 0:w], w), ALU.mult)
                    dve.drain()
                    v.tensor_reduce(top, scratch, AX, ALU.max)
                    dve.drain()
                    v.tensor_tensor(out, scratch, n3(top, w), ALU.is_equal)
                    dve.drain()

                v.tensor_reduce(small(0), gl, AX, ALU.max)
                dve.drain()
                v.tensor_tensor(ge, gl, n3(small(0), NEG), ALU.subtract)
                first_of(og, gl, small(0), NEG, mg, small(1))
                v.tensor_scalar(mg, og, -NEGV, NEGV, ALU.mult, ALU.add)
                by_group = lambda x: x.rearrange("p i (g e) -> p i g e", e=EPG)
                for i in range(nt):
                    v.tensor_tensor(by_group(em)[:, i], by_group(el)[:, i],
                                    og[:, i, :].unsqueeze(2).broadcast_to([P, NEG, EPG]), ALU.mult)
                dve.drain()
                for i in range(nt):
                    v.tensor_tensor(by_group(em)[:, i], by_group(em)[:, i],
                                    mg[:, i, :].unsqueeze(2).broadcast_to([P, NEG, EPG]), ALU.add)
                dve.drain()
                v.tensor_reduce(small(4), em, AX, ALU.max)
                dve.drain()
                first_of(OH[:, 0, 0:nt, :], em, small(4), NEXP, eq, small(1))
                v.scalar_tensor_tensor(out=scr, in0=OH[:, 0, 0:nt, :], scalar=2 * NEGV, in1=em,
                                       op0=ALU.mult, op1=ALU.add)
                dve.drain()
                v.tensor_reduce(small(5), scr, AX, ALU.max)
                dve.drain()
                v.tensor_tensor(small(2), small(5), small(4), ALU.subtract).then_inc(to_exp.sem, 1)
                first_of(OH[:, 1, 0:nt, :], scr, small(5), NEXP, eq, small(1))
                v.tensor_tensor(OHS[:, 0:nt, :], OH[:, 0, 0:nt, :], OH[:, 1, 0:nt, :], ALU.add).then_inc(oh_ready.sem, 1)
                exped.wait(dve, 1)
                v.tensor_reduce(small(6), ge, AX, ALU.add)
                v.tensor_scalar(small(7), small(3), 1.0, None, ALU.add)
                dve.drain()
                v.tensor_tensor(small(6), small(6), small(7), ALU.mult)
                dve.drain()
                v.reciprocal(R.gate[:, 0, 0:nt], small(6))
                dve.drain()
                v.tensor_tensor(R.gate[:, 1, 0:nt], R.gate[:, 0, 0:nt], small(3), ALU.mult)
                rank_ready.wait(dve, 1)
                v.tensor_copy(CE[:, 0, :], ps[:, 4, 256:256 + NEXP])
                v.tensor_copy(scr, ps[:, 4, 0:nt * NEXP].rearrange("p (i n) -> p i n", n=NEXP))
                v.memset(CE[:, 3, :], 1.0)
                dve.drain()
                v.tensor_tensor(CB[:, :, :], CE[:, 0, :].unsqueeze(2).broadcast_to([P, NEXP, 8]),
                                caps.unsqueeze(1).broadcast_to([P, NEXP, 8]), ALU.is_gt)
                dve.drain()
                v.tensor_reduce(CE[:, 1, :], CB[:, :, :], AX, ALU.add)
                dve.drain()
                v.tensor_tensor_scan(CE[:, 2, :], CE[:, 3, :], CE[:, 1, :], 0.0, ALU.mult, ALU.add)
                dve.drain()
                v.tensor_tensor(CE[:, 0, :], CE[:, 2, :], CE[:, 1, :], ALU.subtract)
                v.tensor_tensor(OB[:, :, :], CE[:, 2, :].unsqueeze(1).broadcast_to([P, NOVF, NEXP]),
                                bidx.unsqueeze(2).broadcast_to([P, NOVF, NEXP]), ALU.is_le)
                dve.drain()
                v.tensor_reduce(CB[:, 0:2, :].rearrange("p a b -> p (a b)"), OB[:, :, :], AX, ALU.add)
                dve.drain()
                v.tensor_scalar(R.plan[:, 1:1 + NOVF], CB[:, 0:2, :].rearrange("p a b -> p (a b)"), NEXP - 1.0, None, ALU.min)
                v.tensor_scalar(R.plan[:, 0:1], CE[:, 2, NEXP - 1:NEXP], 1.0, None, ALU.max)
                for k in range(2):
                    for src, to in ((scr, 8), (row(idx32, NEXP), 9), (row(CE[:, 0, :], NEXP), 10)):
                        v.tensor_tensor(eq, OH[:, k, 0:nt, :], src, ALU.mult)
                        dve.drain()
                        v.tensor_reduce(small(to, k), eq, AX, ALU.add)
                        dve.drain()
                    b, jb = small(11, k), JB[:, 0:nt, :]
                    v.tensor_tensor(jb, n3(small(8, k), 8), row(caps, 8), ALU.is_ge)
                    dve.drain()
                    v.tensor_reduce(b, jb, AX, ALU.add)
                    dve.drain()
                    v.scalar_tensor_tensor(out=small(10, k), in0=small(10, k), scalar=NEXP - 1.0, in1=b,
                                           op0=ALU.add, op1=ALU.add)
                    v.tensor_scalar(small(7, k), b, 1.0, None, ALU.min)
                    dve.drain()
                    v.tensor_tensor(small(10, k), small(10, k), small(9, k), ALU.subtract)
                    dve.drain()
                    v.tensor_tensor(small(10, k), small(10, k), small(7, k), ALU.mult)
                    dve.drain()
                    v.tensor_tensor(small(10, k), small(10, k), small(9, k), ALU.add)
                    dve.drain()
                    v.tensor_tensor(small(10, k), small(10, k), b, ALU.subtract)
                    dve.drain()
                    last = v.scalar_tensor_tensor(out=R.slot[:, k, 0:nt], in0=small(10, k), scalar=float(CAP),
                                                  in1=small(8, k), op0=ALU.mult, op1=ALU.add)
                last.then_inc(slots_ready.sem, 1)
                tab_turned.wait(dve, 1)
                v.tensor_copy(R.index[:, 0:NBLK], ps[0:CAP, 5, 0:NBLK])
        consts.passed(16 * 5)
        row_ready.passed(2 * nt)
        row_out.passed(2 * nt)
        stored.passed(16 * nt)
        zeroed.passed(16)
        scattered.passed(16 * 2 * nt)
        tab_in.passed(16)
        for s in (logit_ready, to_exp, exped, oh_ready, rank_ready, slots_ready, tab_turned, zt):
            s.passed(1)


class Routing:

    def __init__(self, c, ctx, l):
        def sb(name, shape, dt):
            return ctx.enter_context(c.nc.sbuf_tensor(f"{name}_{l}", shape, dt))
        self.slot, self.gate = sb("slots", [P, 2, TT], U32), sb("expert_gates", [P, 2, TT], F32)
        self.index, self.plan = sb("slot_index", [CAP, NBLK], U32), sb("overflow_plan", [P, 1 + NOVF], U32)


def experts(c, l, R):
    nc, ps, ring = c.nc, c.ps, c.ring
    with ExitStack() as ctx:
        def sb(name, shape, dt=F32):
            return ctx.enter_context(nc.sbuf_tensor(f"{name}_{l}", shape, dt))

        IDX = sb("gather_index", [CAP, 2], U32)
        XS, XT = sb("slot_rows", [CAP, 2, D]), sb("slot_rows_turned", [P, 2, KT, CAP])
        SG, HT, YS = sb("expert_silu", [P, 4, CAP]), sb("expert_hidden", [P, 4, CAP]), sb("expert_rows", [CAP, 2, D])

        for part in ("first", "more"):
            more = part == "more"
            sg = lambda n: c.sig(f"moe_{n}") if not more else Signal(c.sem(f"more{l}_{n}"))
            gathered = [sg("gathered0"), sg("gathered1")]
            x_turned, x_copied = sg("x_turned"), sg("x_copied")
            w1_done, w3_done, silu, hidden = sg("w1_done"), sg("w3_done"), sg("silu_ready"), sg("hidden_ready")
            y_done, y_act, y_dve = sg("y_done"), sg("y_copied_act"), sg("y_copied_dve")
            y_out = [sg("y_stored0"), sg("y_stored1")]
            landed = Signal(c.sem(f"more{l}_weights")) if more else None
            PER = 1 if more else 2
            if more or l == 0:
                prime(c, [x_turned, x_copied, hidden, y_done, y_act, y_dve] + y_out)
            with nc.Block() as block:

                def loop(eng):
                    if more:
                        return eng.Fori(0, eng.value_load(R.plan[0:1, 0:1], min_val=1, max_val=NOVF))
                    return eng.Fori(0, NEXP // 2)

                @block.gpsimd
                def _(pool):
                    with loop(pool) as it:
                        for q in range(PER):
                            blk = it + NEXP if more else it * 2 + q
                            x_turned.wait(pool, it if more else it * 2)
                            nc.gpsimd.tensor_copy(IDX[:, q:q + 1], R.index[:, bass.ds(blk, 1)])
                            pool.drain()
                            pool.indirect_dma_start(XS[:, q, :], None, c.tokens,
                                                    bass.IndirectOffsetOnAxis(IDX[:, q:q + 1], 0))\
                                .then_inc(gathered[q].sem, 16)
                            gathered[q].wait(pool, it * 16 + 16)

                @block.tensor
                def _(pe):
                    base = ring.uses
                    with loop(pe) as it:
                        for q in range(PER):
                            n = it * PER + q
                            gathered[q].wait(pe, it * 16 + 16)
                            x_copied.wait(pe, n)
                            for k in range(KT):
                                last = nc.tensor.transpose(ps[:, k // 4, (k % 4) * CAP:(k % 4 + 1) * CAP],
                                                           XS[:, q, k::KT], c.ident[0:CAP, 0:CAP])
                            last.then_inc(x_turned.sem, 1)
                            x_copied.wait(pe, n + 1)
                            for m, done in enumerate((w1_done, w3_done)):
                                slot = m if more else (base + 3 * q + m) % ring.SLOTS
                                if more:
                                    landed.wait(pe, it * 48 + 48)
                                    if m == 0:
                                        hidden.wait(pe, n)
                                else:
                                    hidden.wait(pe, n)
                                    pe.wait_ge(ring.landed[slot], (it + ((base + 3 * q + m) // ring.SLOTS + 1)) * 16)
                                w = ring.buf[:, slot, :].rearrange("p (k n) -> p k n", k=KT)
                                for j in range(4):
                                    for k in range(KT):
                                        last = nc.tensor.matmul(ps[:, 2 + m, j * CAP:(j + 1) * CAP],
                                                                w[:, k, j * P:(j + 1) * P], XT[:, q, k, :],
                                                                start=(k == 0), stop=(k == KT - 1))
                                last.then_inc(done.sem, 1)
                            hidden.wait(pe, n + 1)
                            y_act.wait(pe, n)
                            y_dve.wait(pe, n)
                            slot = 2 if more else (base + 3 * q + 2) % ring.SLOTS
                            if not more:
                                pe.wait_ge(ring.landed[slot], (it + ((base + 3 * q + 2) // ring.SLOTS + 1)) * 16)
                            w = ring.buf[:, slot, :].rearrange("p (j n) -> p j n", j=4)
                            for h in range(2):
                                for j in range(4):
                                    last = nc.tensor.matmul(ps[0:CAP, 4 + h, :], HT[:, j, :],
                                                            w[:, j, 512 * h:512 * (h + 1)],
                                                            start=(j == 0), stop=(j == 3))
                            last.then_inc(y_done.sem, 1)
                    if not more:
                        ring.uses += 3 * NEXP

                @block.scalar
                def _(act):
                    with loop(act) as it:
                        for q in range(PER):
                            n, blk = it * PER + q, (it + NEXP if more else it * 2 + q)
                            w1_done.wait(act, n + 1)
                            nc.scalar.activation(SG[:, :, :], ps[:, 2, 0:4 * CAP].rearrange("p (j s) -> p j s", j=4),
                                                 ACT.Silu).then_inc(silu.sem, 1)
                            y_done.wait(act, n + 1)
                            y_out[q].wait(act, it * 16)
                            nc.scalar.copy(YS[:, q, 0:512], ps[0:CAP, 4, :]).then_inc(y_act.sem, 1)
                            y_act.wait(act, n + 1)
                            y_dve.wait(act, n + 1)
                            act.dma_start(c.expert_out.rearrange("(b s) d -> b s d", s=CAP)[bass.ds(blk, 1)]
                                          .rearrange("b s d -> s (b d)"), YS[:, q, :]).then_inc(y_out[q].sem, 16)
                            if more:
                                y_out[q].wait(act, it * 16 + 16)
                    if not more:
                        for q in range(2):
                            y_out[q].wait(act, 16 * NEXP // 2)

                @block.vector
                def _(dve):
                    with loop(dve) as it:
                        for q in range(PER):
                            n = it * PER + q
                            x_turned.wait(dve, n + 1)
                            nc.vector.tensor_copy(XT[:, q, :, :].rearrange("p (a k) s -> p a (k s)", a=2),
                                                  ps[:, 0:2, 0:4 * CAP]).then_inc(x_copied.sem, 1)
                            silu.wait(dve, n + 1)
                            w3_done.wait(dve, n + 1)
                            y_done.wait(dve, n)
                            nc.vector.tensor_tensor(HT[:, :, :], SG[:, :, :],
                                                    ps[:, 3, 0:4 * CAP].rearrange("p (j s) -> p j s", j=4),
                                                    ALU.mult).then_inc(hidden.sem, 1)
                            y_done.wait(dve, n + 1)
                            y_out[q].wait(dve, it * 16)
                            nc.vector.tensor_copy(YS[:, q, 512:D], ps[0:CAP, 5, :]).then_inc(y_dve.sem, 1)

                @block.sync
                def _(sp):
                    if not more:
                        base = ring.loads
                        with sp.Fori(0, NEXP // 2 - 1) as it:
                            for q in range(2):
                                for m, (src, done) in enumerate(zip(expert_chunks(c.ios, l, it * 2 + (2 + q)),
                                                                    (w1_done, w3_done, y_done))):
                                    slot = (base + 3 * q + m) % ring.SLOTS
                                    done.wait(sp, it * 2 + q + 1)
                                    sp.dma_start(ring.buf[:, slot, :].rearrange("p (a b) -> p a b", a=src.shape[1]),
                                                 src).then_inc(ring.landed[slot], 16)
                        for n in range(ring.loads, ring.loads + 3 * (NEXP - 2)):
                            assert n < len(ring.chunks)
                        ring.loads += 3 * (NEXP - 2)
                        for n in range(6):
                            ring.last_use[ring.uses - 6 + n] = (y_done.sem, y_done.base + NEXP)
                    else:
                        with loop(sp) as it:
                            expert = sp.value_load(R.plan[0:1, bass.ds(it + 1, 1)], min_val=0, max_val=NEXP - 1)
                            y_done.wait(sp, it)
                            for m, src in enumerate(expert_chunks(c.ios, l, expert)):
                                sp.dma_start(ring.buf[:, m, :].rearrange("p (a b) -> p a b", a=src.shape[1]),
                                             src).then_inc(landed.sem, 16)
            if not more:
                for s in gathered + y_out:
                    s.passed(16 * NEXP // 2)
                for s in (x_turned, x_copied, w1_done, w3_done, silu, hidden, y_done, y_act, y_dve):
                    s.passed(NEXP)


def combine(c, l, R, nt, parts):
    nc, ps, X = c.nc, c.ps, c.X
    with ExitStack() as ctx:
        def sb(name, shape):
            return ctx.enter_context(nc.sbuf_tensor(f"{name}_{l}", shape, F32))

        Y1, Y2, YC = sb("choice1_rows", [P, 2, D]), sb("choice2_rows", [P, 2, D]), sb("combined", [P, TT, D])
        Z = sb("moe_out", [P, 4, S])
        rows_in = [c.sig("combine_rows_landed0"), c.sig("combine_rows_landed1")]
        combined, z_ready = c.sig("combine_done"), c.sig("combine_turned")
        z_read, added = c.sig("combine_scaled"), c.sig("combine_added")
        pieces = [(k, v, at, n) for k in range(KT) for v, (at, n) in enumerate(parts)]
        with nc.Block() as block:

            @block.gpsimd
            def _(pool):
                for i in range(nt):
                    if i >= 2:
                        combined.wait(pool, i - 1)
                    for k, dst in enumerate((Y1, Y2)):
                        pool.indirect_dma_start(dst[:, i % 2, :], None, c.expert_out,
                                                bass.IndirectOffsetOnAxis(R.slot[:, k, i:i + 1], 0))\
                            .then_inc(rows_in[i % 2].sem, 16)

            @block.vector
            def _(dve):
                v = nc.vector
                for i in range(nt):
                    rows_in[i % 2].wait(dve, 32 * (i // 2 + 1))
                    v.tensor_scalar(YC[:, i, :], Y1[:, i % 2, :], R.gate[:, 0, i:i + 1], None, ALU.mult)
                    dve.drain()
                    v.scalar_tensor_tensor(out=YC[:, i, :], in0=Y2[:, i % 2, :], scalar=R.gate[:, 1, i:i + 1],
                                           in1=YC[:, i, :], op0=ALU.mult, op1=ALU.add).then_inc(combined.sem, 1)
                for u, (tile, vv, at, n) in enumerate(pieces):
                    z_read.wait(dve, u + 1)
                    x = X[:, tile, at:at + n]
                    v.scalar_tensor_tensor(out=x, in0=x, scalar=ALPHA, in1=Z[:, u % 4, 0:n],
                                           op0=ALU.mult, op1=ALU.add).then_inc(added.sem, 1)

            @block.tensor
            def _(pe):
                combined.wait(pe, nt)
                for u, (tile, vv, at, n) in enumerate(pieces):
                    if u >= 8:
                        z_read.wait(pe, u - 7)
                    for i in range(at // P, (at + n) // P):
                        last = nc.tensor.transpose(ps[:, u % 8, i * P - at:(i + 1) * P - at],
                                                   YC[:, i, tile * P:(tile + 1) * P], c.ident[:, :])
                    last.then_inc(z_ready.sem, 1)

            @block.scalar
            def _(act):
                for u, (tile, vv, at, n) in enumerate(pieces):
                    z_ready.wait(act, u + 1)
                    if u >= 4:
                        added.wait(act, u - 3)
                    nc.scalar.activation(Z[:, u % 4, 0:n], ps[:, u % 8, 0:n], ACT.Copy,
                                         scale=c.mod[:, l, 40 + tile, vv:vv + 1]).then_inc(z_read.sem, 1)

            @block.sync
            def _(sp):
                c.ring.feed(sp, c.ring.uses + Ring.SLOTS)
        for q in range(2):
            rows_in[q].passed(32 * (nt // 2))
        combined.passed(nt)
        for s in (z_ready, z_read, added):
            s.passed(len(pieces))


def second_block(c):
    nc = c.nc
    c.mod = c.sb("modulations", [P, NL, 48, 2])
    modulations(c)
    for l in range(NL):
        both, seq = [(0, S), (S, C)], [(0, S)]
        parts = both if l < NL - 1 else seq
        with ExitStack() as ctx:
            def sb(name, shape, stack=ctx):
                return stack.enter_context(nc.sbuf_tensor(f"{name}_{l}", shape, F32))
            MIX, K, VG = sb("mix2", [P, KT, T]), sb("keys2", [P, T]), sb("values_gv", [P, TT, NPIECE])
            with ExitStack() as inner:
                HX = sb("modulated", [P, KT, T], inner)
                modulate(c, l, 0, HX, both)
                mixer_inputs(c, l, HX, MIX, K, VG, parts)
            window_attention(c, l, MIX, K, VG)
            mixer_project(c, l, MIX, parts)
        nt = sum(n for _, n in parts) // P
        layer_norm(c, nt * P, f"ln1_g{l}", f"ln1_b{l}")
        with ExitStack() as ctx:
            R = Routing(c, ctx, l)
            with ExitStack() as inner:
                HX = inner.enter_context(nc.sbuf_tensor(f"moe_in_{l}", [P, KT, T], F32))
                modulate(c, l, 3, HX, parts)
                route(c, l, HX, R, nt)
            experts(c, l, R)
            combine(c, l, R, nt, parts)
        layer_norm(c, nt * P, f"ln2_g{l}", f"ln2_b{l}")
    done = c.sem("out_stored")
    with nc.Block(no_gpsimd_drain=True) as block:

        @block.sync
        def _(sp):
            sp.dma_start(c.ios["outT"].rearrange("(k p) t -> p k t", p=P), c.X[:, :, 0:S]).then_inc(done, 16)
            sp.wait_ge(done, 16)


def second_arrays(np_, a, arrays, tiles):
    g = lambda n: a[n + "_2"]
    heads = lambda w: np_.stack([w.reshape(w.shape[:-1] + (H2, HD))[..., h, :] for h in H2_ORDER], -2).reshape(w.shape)
    split = np_.cumsum([512, 128, 128, 256, 256, 256, 256])
    w_in, w_nat, w_out = [], [], []
    for l in range(NL):
        q, k, v, cb, cc, cx, gu, gv = np_.split(g("w_in")[l], split, axis=1)
        w_in.append(tiles(np_.concatenate([heads(q), k, cc, gu[:, :P], cx, cb, gu[:, P:]], 1)))
        w_nat.append(np_.concatenate([v, gv], 1))
        w = g("w_out")[l]
        w_out.append(tiles(np_.concatenate([heads(w[:512].T).T, w[512:]], 0)))
    freqs = (10000.0 ** (-np_.arange(16, dtype=np_.float32) / 16)).astype(np_.float32)
    d = np_.arange(P) % 64
    pos = np_.where((d < 32)[:, None], np_.arange(S)[None, :] // 64, np_.arange(S)[None, :] % 64).astype(np_.float32)
    ang = (pos * freqs[d % 16][:, None]).astype(np_.float32)
    rot = np_.zeros((P, P), np_.float32)
    for m in range(P):
        if m % 32 < 16:
            rot[m + 16, m] = -1.0
        else:
            rot[m - 16, m] = 1.0
    qq, kk = np_.arange(P)[:, None], np_.arange(P)[None, :]
    local = np_.concatenate([np_.where(kk >= qq, 0, NEGV), np_.zeros((P, P)), np_.where(kk <= qq, 0, NEGV)], 1)
    consts = np_.zeros((P, 96), np_.float32)
    consts[:, 0:32] = 32 - np_.arange(32)
    consts[:, 32:64] = np_.arange(32)
    consts[:, 64:72] = CAP * np_.arange(1, 9)
    consts[:, 72:72 + NOVF] = np_.arange(NOVF)
    arrays.update({
        "ctxT": g("ctx")[0].T, "zeros": np_.zeros((1, D), np_.float32),
        "cond": np_.stack([g("c")[0].reshape(KT, P).T, g("c_ctx").reshape(KT, P).T], -1),
        "b_ada": g("b_ada").reshape(NL * 48, P).T,
        "w_ada": np_.concatenate([tiles(g("w_ada")[l]) for l in range(NL)]),
        "w_in2": np_.concatenate(w_in), "w_nat2": np_.stack(w_nat), "w_out2": np_.concatenate(w_out),
        "rope_cos": np_.cos(ang), "rope_sin": np_.sin(ang), "rope_rot": rot,
        "gm_w": g("gm_ws").transpose(0, 3, 1, 2),
        "gm_b": np_.repeat(g("gm_bs").reshape(NL, 2, 2, P).transpose(0, 2, 1, 3), 64, axis=1),
        "conv2": g("conv_w").reshape(NL, 3, 2, P).transpose(0, 3, 2, 1),
        "win_mask": np_.concatenate([local, np_.zeros((P, C)), local], 1).astype(np_.float32),
        "sink": np_.broadcast_to(g("attn_sink")[:, None, H2_ORDER], (NL, P, H2)),
        "w_router": np_.concatenate([g("w_rg"), g("w_re")], 2),
        "b_router": np_.broadcast_to(np_.concatenate([g("b_rg"), g("b_re")], 1)[:, None, :], (NL, P, RW)),
        "earlier": (qq < kk).astype(np_.float32),
        "router_consts": consts,
        "token_ids": (np_.arange(TT)[None, :] * P + np_.arange(P)[:, None]).astype(np_.float32),
        "w1": g("w1").reshape(NL * NEXP, D, DE), "w3": g("w3").reshape(NL * NEXP, D, DE),
        "w2": g("w2").reshape(NL * NEXP, DE, D),
    })


def chunk_list(ios):
    def tiles(name, at, n):
        return ios[name][at:at + n].rearrange("t p w -> p t w")

    out = [tiles("w_rnn", 3 * j, 3) for j in range(KT)]
    out += [tiles("w_att", 0, 4), tiles("w_att", 4, 4)]
    out += [ios["w_values"].rearrange("(k p) n -> p k n", p=P)]
    out += [tiles("w_att", 8, 4), tiles("w_att", 12, 4)]
    out += [ios["cmp_k_w1"].rearrange("(l p) n -> p l n", p=P), ios["cmp_v_w1"].rearrange("(l p) n -> p l n", p=P)]
    out += [tiles("w_att", 16, 4), tiles("w_att", 20, 4)]
    out += [tiles("w_mix_out", 0, 4), tiles("w_mix_out", 4, 4)]
    out += [tiles("w_ffn", 4 * j, 4) for j in range(FT // 2)]
    out += [tiles("w_down", j, 1) for j in range(KT)]
    out += [tiles("w_ple_gate", 0, 4), tiles("w_ple_gate", 4, 4), tiles("w_ple_proj", 0, KT)]
    return out + second_chunks(ios)


def build_program(nc, ios):
    with ExitStack() as ctx:
        c = Core()
        c.nc, c.ios = nc, ios

        def sb(name, shape, dt=F32):
            return ctx.enter_context(nc.sbuf_tensor(name, shape, dt))

        def sem(name):
            return ctx.enter_context(nc.semaphore(name))

        c.sem = sem
        c.sb = sb
        c.ring = Ring(nc, ctx, chunk_list(ios))
        c.ps = ctx.enter_context(nc.psum_tensor("psum", [P, 8, 512], F32))
        c.X = sb("residual", [P, KT, T])
        c.ones, c.ident = sb("ones", [P, 1]), sb("identity", [P, P])
        c.vecs = sb("vectors", [P, len(VECS), KT])
        c.slopes = sb("alibi_slopes", [P, NHEAD])
        c.vec = lambda name, k: c.vecs[:, VECS.index(name), k:k + 1]
        c.x_landed, c.consts_landed = sem("x_landed"), sem("consts_landed")
        c.w2_landed, c.out_read = sem("cmp_w2_landed"), sem("ffn_out_read")
        c.ph = [Signal(sem(f"{name}")) for name in
                ("stage_squares_or_tiles", "stage_partial_sums", "stage_means", "stage_inverse")]
        c.const_loads = [(c.ident[:, :], ios["ident"]), (c.vecs[:, :, :], ios["vecs"]),
                         (c.slopes[:, :], ios["slopes"])]
        second_setup(c)
        with ExitStack() as first:
            def fsb(name, shape, stack=first):
                return stack.enter_context(nc.sbuf_tensor(name, shape, F32))
            c.H = fsb("normed", [P, KT, S])
            with ExitStack() as mixers:
                c.Y = fsb("mixed", [P, KT, S], mixers)
                with stat_buffers(c):
                    norm_and_start(c, ios)
                recurrent_mixer(c)
                with ExitStack() as att:
                    c.Q, c.KK = fsb("queries", [P, KT, S], att), fsb("keys", [P, 4, S], att)
                    c.G = fsb("gates", [P, ST, 3 * NHEAD], att)
                    c.KCC, c.VCC = fsb("cmp_keys", [P, 64], att), fsb("cmp_values", [P, HD], att)
                    c.V = lambda i: c.X[:, :, S:T].rearrange("p (b i) n -> p i b n", b=2)[:, i]
                    c.Vt = lambda br, i: c.X[:, 4 * br + i, S:T]
                    attention_inputs(c)
                    with ExitStack() as pct:
                        c.PCT = fsb("cmp_probs_turned", [P, 4, S], pct)
                        compressed_probs(c)
                        causal_attention(c)
                    mixer_output(c)
                sq = fsb("squares", [P, KT, S], mixers)
                with stat_buffers(c):
                    rms_scale(c, c.H[:, :, :], sq, S)
                    scale_by(c, sq, c.H, "g_mix_post", add_to=c.X[:, :, 0:S])
                    rms_scale(c, c.X[:, :, 0:S], sq, S)
                    scale_by(c, c.H, c.X[:, :, 0:S], "g_ffn_pre")
            Z = fsb("ffn_out", [P, KT, S])
            feed_forward(c, Z)
            with stat_buffers(c):
                rms_scale(c, Z[:, :, :], c.H, S)
                scale_by(c, c.H, Z, "g_ffn_post", add_to=c.X[:, :, 0:S])
        per_layer_embedding(c)
        second_block(c)


def kernel(**inputs):
    import numpy as _np
    import concourse.bacc as _bacc
    from concourse import mybir as _mybir
    from concourse.bass_utils import run_bass_kernel_spmd as _run

    a = {k: _np.asarray(v) for k, v in inputs.items()}

    def tiles(w):
        k, f = w.shape
        return _np.ascontiguousarray(w.reshape(k // P, P, f // P, P).transpose(2, 1, 0, 3)).reshape(f // P, P, k)

    def mixed(x):
        blocks = x.reshape(x.shape[:-1] + (NHEAD, HD))
        return _np.stack([blocks[..., b, :] for b in MIX_ORDER], -2).reshape(x.shape)

    def by_partition(v):
        return v.reshape(KT, P).T

    w_in = a["w_in"][0]
    sizes = [D, D, NHEAD * HD] + 6 * [NGRP * HD] + [3 * NHEAD, D, D]
    ends = _np.cumsum(sizes)
    xr, gr, q, kc, vc, ks, vs, kw, vw, gn, gmr, gma = (w_in[:, e - n:e] for e, n in zip(ends, sizes))
    rnn = [tiles(mixed(w)) for w in (xr, gr, gmr)]
    gates = gn.reshape(D, NHEAD, 3)
    by_group = [4 * g + r for r in range(4) for g in range(NGRP)]
    gu = a["ffn_w_gate_up"][0]
    ffn = _np.stack([tiles(gu[:, :FF]), tiles(gu[:, FF:])], 1).reshape(2 * FT, P, D)
    mix_rows = lambda w: mixed(w.T).T
    vec = {
        "g_mix_pre": a["norm_mix_pre"][0], "g_mix_post": a["norm_mix_post"][0],
        "g_ffn_pre": a["norm_ffn_pre"][0], "g_ffn_post": a["norm_ffn_post"][0], "ple_b": a["ple_b_gate"][0],
        "conv_b": mixed(a["conv_b"][0]), "lru_ba": mixed(a["lru_ba"][0]), "lru_bx": mixed(a["lru_bx"][0]),
        "lru_lam": mixed(a["lru_lambda"][0]),
    }
    for t in range(CONV):
        vec[f"conv{t}"] = mixed(a["conv_w"][0, t])
    for l in range(NL):
        for n in ("ln1_g", "ln1_b", "ln2_g", "ln2_b"):
            vec[f"{n}{l}"] = a[n + "_2"][l]

    slopes = _np.exp2(-8.0 * _np.arange(1, NHEAD + 1, dtype=_np.float32) / NHEAD).astype(_np.float32)
    tq, tk = _np.arange(S)[:, None], _np.arange(S)[None, :]
    dist = _np.where(tq >= tk, -(tq - tk), NEGV).astype(_np.float32)
    dc = _np.arange(S)[:, None] - (_np.arange(CPAD)[None, :] * 16 + 31)
    seen = (dc >= 0) & (_np.arange(CPAD)[None, :] < NCMP)
    cmp_bias = _np.where(seen[:, None, :], -slopes[by_group][None, :, None] * dc[:, None, :], NEGV)

    arrays = {
        "xT": a["x"][0].T, "pT": a["p"][0, 0].T,
        "ident": _np.eye(P, dtype=_np.float32),
        "vecs": _np.stack([by_partition(vec[n]) for n in VECS], 1),
        "w_rnn": _np.stack(rnn, 1).reshape(3 * KT, P, D),
        "w_att": _np.concatenate([tiles(kc), tiles(vc), tiles(ks), tiles(kw), tiles(mixed(q)), tiles(mixed(gma))]),
        "w_values": _np.concatenate([vs, vw], 1),
        "w_gates": _np.concatenate([gates[:, by_group, 0], gates[:, MIX_ORDER, 1], gates[:, MIX_ORDER, 2]], 1),
        "cmp_k_w1": a["cmp_k_w1"][0], "cmp_v_w1": a["cmp_v_w1"][0],
        "cmp_k_w2": a["cmp_k_w2"][0], "cmp_v_w2": a["cmp_v_w2"][0],
        "cmp_pos": _np.stack([a[n][0].reshape(16, 2, HD).transpose(1, 2, 0).reshape(P, 16)
                              for n in ("cmp_pos_k", "cmp_pos_v")], 1),
        "lru_wa": a["lru_wa"][0][MIX_ORDER], "lru_wx": a["lru_wx"][0][MIX_ORDER],
        "w_mix_out": tiles(mix_rows(a["w_out"][0])),
        "w_ffn": ffn, "w_down": tiles(a["ffn_w_down"][0]),
        "w_ple_gate": tiles(a["ple_w_gate"][0]), "w_ple_proj": tiles(a["ple_w_proj"][0]),
        "causal_dist": dist[S - P:],
        "slopes": _np.broadcast_to(slopes[MIX_ORDER], (P, NHEAD)),
        "cmp_bias": cmp_bias.astype(_np.float32).reshape(ST, P, 512).transpose(1, 0, 2),
        "cmp_mask": seen.astype(_np.float32).reshape(ST, P, CPAD).transpose(1, 0, 2),
    }
    second_arrays(_np, a, arrays, tiles)
    nc = _bacc.Bacc("TRN2", target_bir_lowering=False, num_devices=1)
    maps, ios = {}, {}
    for name, v in arrays.items():
        v = _np.ascontiguousarray(v)
        maps[f"in_{name}_dram"] = v
        ios[name] = nc.dram_tensor(f"in_{name}_dram", v.shape, _mybir.dt.from_np(v.dtype), kind="ExternalInput").ap()
    ios["outT"] = nc.dram_tensor("out_0_dram", (D, S), F32, kind="ExternalOutput").ap()
    build_program(nc, ios)
    r = _run(nc, [maps], core_ids=[0])
    return _np.ascontiguousarray(r.results[0]["out_0_dram"].T)[None]
```
